# Optimizing a Trainium2 kernel written in Bass

```python
import math
import jax, jax.numpy as jnp
from jax import lax
import numpy as np

D_MODEL = 1024
BATCH = 1
SEQ = 512
DEPTH = 2

MIX_WIDTH = D_MODEL
POOL_WIDTH = MIX_WIDTH // 2
POOL_WINDOWS = (2, 4, 8, 16)
POOL_GROUPS = len(POOL_WINDOWS)
POOL_GC = POOL_WIDTH // POOL_GROUPS
N_HEADS = 4
QK_NOPE = 128
QK_ROPE = 64
V_HEAD = 128
QK_HEAD = QK_NOPE + QK_ROPE
MLA_WIDTH = N_HEADS * V_HEAD
Q_LORA = 384
KV_LORA = 256
ROPE_THETA = 10000.0
SOFTMAX_SCALE = 1.0 / math.sqrt(QK_HEAD)
Q_BLOCK = 128
IN_COLS = POOL_WIDTH + Q_LORA + KV_LORA + QK_ROPE
D_FF = 2816
N_SUBLAYERS = 3
EPS = 1e-6


def rms_norm(x, g):
    xf = x.astype(jnp.float32)
    y = xf * lax.rsqrt(jnp.mean(xf * xf, axis=-1, keepdims=True) + EPS)
    return (y * g.astype(jnp.float32)).astype(x.dtype)

def modulate(h, shift, scale):
    return h * (1 + scale[:, None, :]) + shift[:, None, :]

def swiglu(h, w_gate, w_up, w_down):
    return (jax.nn.silu(h @ w_gate) * (h @ w_up)) @ w_down

def rotate_half(x):
    x1, x2 = jnp.split(x, 2, axis=-1)
    return jnp.concatenate([-x2, x1], axis=-1)

def apply_rope(x, cos, sin):
    return x * cos + rotate_half(x) * sin

def causal_multiscale_pool(u, pool_w, pool_scale):
    B, S, C = u.shape
    cs = jnp.cumsum(u.astype(jnp.float32), axis=1)
    pos = jnp.arange(S)
    means = []
    for g, w in enumerate(POOL_WINDOWS):
        csg = cs[..., g * POOL_GC:(g + 1) * POOL_GC]
        lag = jnp.pad(csg, ((0, 0), (w, 0), (0, 0)))[:, :S]
        cnt = jnp.minimum(pos + 1, w).astype(jnp.float32)[None, :, None]
        means.append((csg - lag) / cnt)
    pooled = jnp.stack(means, axis=2).astype(u.dtype)
    diff = pooled - u.reshape(B, S, POOL_GROUPS, POOL_GC)
    y = jnp.einsum('bsgc,gcd->bsgd', diff, pool_w).reshape(B, S, C)
    return y * pool_scale

def mla_attention(cq, ckv, kr, q_a_norm, w_q_b, kv_a_norm, w_kv_b, cos, sin):
    B, S, _ = cq.shape
    q = (rms_norm(cq, q_a_norm) @ w_q_b).reshape(B, S, N_HEADS, QK_HEAD)
    q_nope, q_rope = q[..., :QK_NOPE], q[..., QK_NOPE:]
    q_rope = apply_rope(q_rope, cos[:, :, None, :], sin[:, :, None, :])
    kv = (rms_norm(ckv, kv_a_norm) @ w_kv_b).reshape(B, S, N_HEADS, QK_NOPE + V_HEAD)
    k_nope, v = kv[..., :QK_NOPE], kv[..., QK_NOPE:]
    k_rope = apply_rope(kr, cos, sin)

    nb = S // Q_BLOCK
    qn = q_nope.reshape(B, nb, Q_BLOCK, N_HEADS, QK_NOPE).transpose(1, 0, 3, 2, 4)
    qr = q_rope.reshape(B, nb, Q_BLOCK, N_HEADS, QK_ROPE).transpose(1, 0, 3, 2, 4)
    kn = k_nope.transpose(0, 2, 1, 3)
    vv = v.transpose(0, 2, 1, 3)
    kpos = jnp.arange(S)

    def block(args):
        qn_b, qr_b, i = args
        s = (jnp.einsum('bhqd,bhkd->bhqk', qn_b, kn)
             + jnp.einsum('bhqd,bkd->bhqk', qr_b, k_rope)).astype(jnp.float32) * SOFTMAX_SCALE
        qpos = i * Q_BLOCK + jnp.arange(Q_BLOCK)
        s = jnp.where(qpos[:, None] >= kpos[None, :], s, -jnp.inf)
        p = jax.nn.softmax(s, axis=-1).astype(vv.dtype)
        return jnp.einsum('bhqk,bhkd->bhqd', p, vv)

    o = lax.map(block, (qn, qr, jnp.arange(nb)))
    return o.transpose(1, 0, 3, 2, 4).reshape(B, S, MLA_WIDTH)

def first_inputs(seed: int = 0) -> dict:
    key = jax.random.key(seed)
    ks = jax.random.split(key, 24)
    f32 = jnp.float32
    nrm = lambda k, shape, s: (jax.random.normal(k, shape, f32) * s)
    gain = lambda k, shape: 1.0 + 0.05 * jax.random.normal(k, shape, f32)
    D, F, L = D_MODEL, D_FF, DEPTH
    x = jax.random.normal(ks[0], (BATCH, SEQ, D), f32)
    c = jax.random.normal(ks[1], (BATCH, D), f32)
    positions = jnp.broadcast_to(jnp.arange(SEQ, dtype=jnp.int32)[None, :], (BATCH, SEQ))
    return {
        "x": x,
        "c": c,
        "positions": positions,
        "ada_w": nrm(ks[2], (L, D, 3 * N_SUBLAYERS * D), 0.5 * D ** -0.5),
        "ada_b": nrm(ks[3], (L, 3 * N_SUBLAYERS * D), 0.01),
        "ffn1_norm": gain(ks[4], (L, D)),
        "ffn1_w_gate": nrm(ks[5], (L, D, F), D ** -0.5),
        "ffn1_w_up": nrm(ks[6], (L, D, F), D ** -0.5),
        "ffn1_w_down": nrm(ks[7], (L, F, D), F ** -0.5),
        "mix_norm": gain(ks[8], (L, D)),
        "w_in": nrm(ks[9], (L, D, IN_COLS), D ** -0.5),
        "pool_w": nrm(ks[10], (L, POOL_GROUPS, POOL_GC, POOL_GC), POOL_GC ** -0.5),
        "pool_scale": gain(ks[11], (L, POOL_WIDTH)),
        "q_a_norm": gain(ks[12], (L, Q_LORA)),
        "w_q_b": nrm(ks[13], (L, Q_LORA, N_HEADS * QK_HEAD), Q_LORA ** -0.5),
        "kv_a_norm": gain(ks[14], (L, KV_LORA)),
        "w_kv_b": nrm(ks[15], (L, KV_LORA, N_HEADS * (QK_NOPE + V_HEAD)), KV_LORA ** -0.5),
        "w_out": nrm(ks[16], (L, MIX_WIDTH, D), MIX_WIDTH ** -0.5),
        "ffn2_norm": gain(ks[17], (L, D)),
        "ffn2_w_gate": nrm(ks[18], (L, D, F), D ** -0.5),
        "ffn2_w_up": nrm(ks[19], (L, D, F), D ** -0.5),
        "ffn2_w_down": nrm(ks[20], (L, F, D), F ** -0.5),
        "final_norm": gain(ks[21], (D,)),
    }

def first_block(x, c, positions, ada_w, ada_b, ffn1_norm, ffn1_w_gate, ffn1_w_up, ffn1_w_down,
              mix_norm, w_in, pool_w, pool_scale, q_a_norm, w_q_b, kv_a_norm, w_kv_b, w_out,
              ffn2_norm, ffn2_w_gate, ffn2_w_up, ffn2_w_down, final_norm):
    inv_freq = 1.0 / (ROPE_THETA ** (jnp.arange(0, QK_ROPE, 2, dtype=jnp.float32) / QK_ROPE))
    ang = positions.astype(jnp.float32)[..., None] * inv_freq
    ang = jnp.concatenate([ang, ang], axis=-1)
    cos = jnp.cos(ang).astype(x.dtype)
    sin = jnp.sin(ang).astype(x.dtype)
    c_act = jax.nn.silu(c)

    for l in range(DEPTH):
        mod = c_act @ ada_w[l] + ada_b[l]
        (sh1, sc1, g1, sh2, sc2, g2, sh3, sc3, g3) = jnp.split(mod, 3 * N_SUBLAYERS, axis=-1)

        h = modulate(rms_norm(x, ffn1_norm[l]), sh1, sc1)
        x = x + 0.5 * g1[:, None, :] * swiglu(h, ffn1_w_gate[l], ffn1_w_up[l], ffn1_w_down[l])

        h = modulate(rms_norm(x, mix_norm[l]), sh2, sc2)
        z = h @ w_in[l]
        o1 = POOL_WIDTH
        o2 = o1 + Q_LORA
        o3 = o2 + KV_LORA
        y_pool = causal_multiscale_pool(z[..., :o1], pool_w[l], pool_scale[l])
        y_mla = mla_attention(z[..., o1:o2], z[..., o2:o3], z[..., o3:], q_a_norm[l], w_q_b[l],
                              kv_a_norm[l], w_kv_b[l], cos, sin)
        y = jnp.concatenate([y_pool, y_mla], axis=-1) @ w_out[l]
        x = x + g2[:, None, :] * y

        h = modulate(rms_norm(x, ffn2_norm[l]), sh3, sc3)
        x = x + 0.5 * g3[:, None, :] * swiglu(h, ffn2_w_gate[l], ffn2_w_up[l], ffn2_w_down[l])

    return rms_norm(x, final_norm)


DEPTH_2 = 1

CTX_LEN = 256
GRID_W = 64
MIX_WIDTH_2 = 2 * D_MODEL
SSD_DINNER = MIX_WIDTH_2 // 2
SSD_HEADDIM = 64
SSD_HEADS = SSD_DINNER // SSD_HEADDIM
SSD_GROUPS = 2
SSD_STATE = 64
SSD_CHUNK = 128
SSD_CONV_CH = SSD_DINNER + 2 * SSD_GROUPS * SSD_STATE
GDN_WIDTH = MIX_WIDTH_2 - SSD_DINNER
GDN_HEADDIM = 128
GDN_HEADS = GDN_WIDTH // GDN_HEADDIM
GDN_CHUNK = 64
GDN_CONV_CH = 3 * GDN_WIDTH
CONV_K = 5
N_DIR = 2
D_FF_2 = 4 * D_MODEL
IN_SIZES = (SSD_DINNER, SSD_CONV_CH, N_DIR * SSD_HEADS, GDN_CONV_CH, GDN_WIDTH, N_DIR * GDN_HEADS, N_DIR * GDN_HEADS)
IN_DIM = sum(IN_SIZES)


def rmsnorm(x, g):
    xf = x.astype(jnp.float32)
    y = xf * lax.rsqrt(jnp.mean(xf * xf, axis=-1, keepdims=True) + EPS)
    return y.astype(x.dtype) * g

def l2norm(x):
    xf = x.astype(jnp.float32)
    return (xf * lax.rsqrt(jnp.sum(xf * xf, axis=-1, keepdims=True) + EPS)).astype(x.dtype)

def modulate_2(h, shift, scale):
    return h * (1.0 + scale) + shift

def dwconv(x, w, b):
    y = lax.conv_general_dilated(x, w[:, None, :].astype(x.dtype), window_strides=(1,),
                                 padding=[(CONV_K // 2, CONV_K // 2)],
                                 dimension_numbers=('NWC', 'WIO', 'NWC'),
                                 feature_group_count=x.shape[-1])
    return y if b is None else y + b

def conv_rows(x, w, b):
    bsz, n, ch = x.shape
    rows = n // GRID_W
    return dwconv(x.reshape(bsz * rows, GRID_W, ch), w, b).reshape(bsz, n, ch)

def split_cols(p):
    parts, start = [], 0
    for size in IN_SIZES:
        parts.append(p[..., start:start + size])
        start += size
    return parts

def _ident(t):
    return t

def _flip(t):
    return jnp.flip(t, axis=1)

def ssd_scan(xh, dt, A, Bm, Cm, h0, return_y):
    bsz, n, H, P = xh.shape
    G, N = Bm.shape[2], Bm.shape[3]
    Q = SSD_CHUNK
    nc = n // Q
    rep = H // G
    x_c = xh.reshape(bsz, nc, Q, H, P)
    dt_c = dt.reshape(bsz, nc, Q, H)
    B_c = jnp.repeat(Bm, rep, axis=2).reshape(bsz, nc, Q, H, N)
    acum = jnp.cumsum(dt_c * A, axis=2)
    xdt = x_c * dt_c[..., None]
    states = jnp.einsum('bcqhn,bcqh,bcqhp->bchpn', B_c, jnp.exp(acum[:, :, -1:] - acum), xdt)
    chunk_decay = jnp.exp(acum[:, :, -1])

    def step(h, inp):
        s, d = inp
        h_next = h * d[:, :, None, None] + s
        return h_next, (h if return_y else None)

    h_final, h_prev = lax.scan(step, h0, (jnp.moveaxis(states, 1, 0), jnp.moveaxis(chunk_decay, 1, 0)))
    if not return_y:
        return None, h_final
    C_c = jnp.repeat(Cm, rep, axis=2).reshape(bsz, nc, Q, H, N)
    h_prev = jnp.moveaxis(h_prev, 0, 1)
    causal = jnp.tril(jnp.ones((Q, Q), bool))
    seg = acum[:, :, :, None, :] - acum[:, :, None, :, :]
    lmat = jnp.exp(jnp.where(causal[:, :, None], seg, -jnp.inf))
    scores = jnp.einsum('bcihn,bcjhn->bcijh', C_c, B_c) * lmat
    y = (jnp.einsum('bcijh,bcjhp->bcihp', scores, xdt)
         + jnp.einsum('bcihn,bchpn->bcihp', C_c, h_prev) * jnp.exp(acum)[..., None])
    return y.reshape(bsz, n, H, P), h_final

def gdn_scan(q, k, v, g, beta, S0, return_y):
    bsz, n, H, K = q.shape
    V = v.shape[-1]
    Q = GDN_CHUNK
    nc = n // Q

    def chunk(t):
        return jnp.swapaxes(t.reshape((bsz, nc, Q) + t.shape[2:]), 2, 3)

    qc, kc, vc = chunk(q), chunk(k), chunk(v)
    gcum = jnp.cumsum(chunk(g), axis=-1)
    bc = chunk(beta)[..., None]
    k_beta = kc * bc
    incl = jnp.tril(jnp.ones((Q, Q), bool))
    strict = jnp.tril(jnp.ones((Q, Q), bool), -1)
    decay = jnp.exp(jnp.where(incl, gcum[..., :, None] - gcum[..., None, :], -jnp.inf))
    kk = jnp.einsum('bchik,bchjk->bchij', k_beta, kc) * decay
    tmat = (jnp.eye(Q, dtype=jnp.float32) + jnp.where(strict, kk, 0.0)).astype(jnp.float32)
    rhs = jnp.concatenate([vc * bc, k_beta * jnp.exp(gcum)[..., None]], axis=-1).astype(jnp.float32)
    sol = lax.linalg.triangular_solve(tmat, rhs, left_side=True, lower=True, unit_diagonal=True)
    u, w = sol[..., :V], sol[..., V:]
    k_dec = kc * jnp.exp(gcum[..., -1:] - gcum)[..., None]
    chunk_decay = jnp.exp(gcum[..., -1])
    xs = [u, w, k_dec, chunk_decay]
    if return_y:
        q_dec = qc * jnp.exp(gcum)[..., None]
        qk = jnp.einsum('bchik,bchjk->bchij', qc, kc) * decay
        xs += [q_dec, qk]
    xs = tuple(jnp.moveaxis(t, 1, 0) for t in xs)

    def step(S, inp):
        u_i, w_i, kd_i, d_i = inp[:4]
        v_new = u_i - jnp.einsum('bhqk,bhkv->bhqv', w_i, S)
        S_next = S * d_i[..., None, None] + jnp.einsum('bhqk,bhqv->bhkv', kd_i, v_new)
        if not return_y:
            return S_next, None
        qd_i, qk_i = inp[4:]
        o = jnp.einsum('bhqk,bhkv->bhqv', qd_i, S) + jnp.einsum('bhij,bhjv->bhiv', qk_i, v_new)
        return S_next, o

    S_final, o = lax.scan(step, S0, xs)
    if not return_y:
        return None, S_final
    o = jnp.swapaxes(jnp.moveaxis(o, 0, 1), 2, 3).reshape(bsz, n, H, V)
    return o, S_final

def ssd_out_norm(y, z, g):
    bsz, n = y.shape[:2]
    v = (y.reshape(bsz, n, SSD_DINNER) * jax.nn.silu(z)).astype(jnp.float32)
    v = v.reshape(bsz, n, SSD_GROUPS, SSD_DINNER // SSD_GROUPS)
    v = v * lax.rsqrt(jnp.mean(v * v, axis=-1, keepdims=True) + EPS)
    return v.reshape(bsz, n, SSD_DINNER) * g

def gdn_out_norm(o, gate, g):
    bsz, n = o.shape[:2]
    return (rmsnorm(o, g) * jax.nn.silu(gate.reshape(bsz, n, GDN_HEADS, GDN_HEADDIM))).reshape(bsz, n, GDN_WIDTH)

def ssd_parts(xbc, dt):
    b_, l_ = xbc.shape[:2]
    xs, bm, cm = jnp.split(xbc, [SSD_DINNER, SSD_DINNER + SSD_GROUPS * SSD_STATE], axis=-1)
    return (xs.reshape(b_, l_, SSD_HEADS, SSD_HEADDIM),
            bm.reshape(b_, l_, SSD_GROUPS, SSD_STATE),
            cm.reshape(b_, l_, SSD_GROUPS, SSD_STATE),
            dt.reshape(b_, l_, N_DIR, SSD_HEADS).astype(jnp.float32))

def gdn_parts(qkv, a, beta):
    b_, l_ = qkv.shape[:2]
    q, k, v = jnp.split(qkv, 3, axis=-1)
    hs = (b_, l_, GDN_HEADS, GDN_HEADDIM)
    q = l2norm(q.reshape(hs)) * (GDN_HEADDIM ** -0.5)
    k = l2norm(k.reshape(hs))
    return (q, k, v.reshape(hs),
            a.reshape(b_, l_, N_DIR, GDN_HEADS).astype(jnp.float32),
            jax.nn.sigmoid(beta.reshape(b_, l_, N_DIR, GDN_HEADS).astype(jnp.float32)))

def token_mixers(p_lat, p_ctx, ssd_conv_w, ssd_conv_b, ssd_dt_bias, ssd_A_log, ssd_D, ssd_norm_g,
                 gdn_conv_w, gdn_dt_bias, gdn_A_log, gdn_norm_g, ctx_out):
    bsz = p_lat.shape[0]
    z_l, xbc_l, dt_l, qkv_l, gate_l, a_l, b_l = split_cols(p_lat)
    z_c, xbc_c, dt_c, qkv_c, gate_c, a_c, b_c = split_cols(p_ctx)
    xbc_l = jax.nn.silu(conv_rows(xbc_l, ssd_conv_w, ssd_conv_b))
    xbc_c = jax.nn.silu(dwconv(xbc_c, ssd_conv_w, ssd_conv_b))
    qkv_l = jax.nn.silu(conv_rows(qkv_l, gdn_conv_w, None))
    qkv_c = jax.nn.silu(dwconv(qkv_c, gdn_conv_w, None))
    xs_l, bm_l, cm_l, dt_l = ssd_parts(xbc_l, dt_l)
    xs_c, bm_c, cm_c, dt_c = ssd_parts(xbc_c, dt_c)
    q_l, k_l, v_l, a_l, be_l = gdn_parts(qkv_l, a_l, b_l)
    q_c, k_c, v_c, a_c, be_c = gdn_parts(qkv_c, a_c, b_c)

    ssd_l = xs_l * ssd_D[:, None]
    gdn_l = 0.0
    if ctx_out:
        ssd_c = xs_c * ssd_D[:, None]
        gdn_c = 0.0
    for d in range(N_DIR):
        o = _ident if d == 0 else _flip
        A = -jnp.exp(ssd_A_log[d].astype(jnp.float32))
        dtc = jax.nn.softplus(dt_c[:, :, d] + ssd_dt_bias[d])
        dtl = jax.nn.softplus(dt_l[:, :, d] + ssd_dt_bias[d])
        h0 = jnp.zeros((bsz, SSD_HEADS, SSD_HEADDIM, SSD_STATE), jnp.float32)
        yc, h_ctx = ssd_scan(o(xs_c), o(dtc), A, o(bm_c), o(cm_c), h0, ctx_out)
        yl, _ = ssd_scan(o(xs_l), o(dtl), A, o(bm_l), o(cm_l), h_ctx, True)
        ssd_l = ssd_l + o(yl)
        rate = jnp.exp(gdn_A_log[d].astype(jnp.float32))
        gc = -rate * jax.nn.softplus(a_c[:, :, d] + gdn_dt_bias[d])
        gl = -rate * jax.nn.softplus(a_l[:, :, d] + gdn_dt_bias[d])
        s0 = jnp.zeros((bsz, GDN_HEADS, GDN_HEADDIM, GDN_HEADDIM), jnp.float32)
        oc, s_ctx = gdn_scan(o(q_c), o(k_c), o(v_c), o(gc), o(be_c[:, :, d]), s0, ctx_out)
        ol, _ = gdn_scan(o(q_l), o(k_l), o(v_l), o(gl), o(be_l[:, :, d]), s_ctx, True)
        gdn_l = gdn_l + o(ol)
        if ctx_out:
            ssd_c = ssd_c + o(yc)
            gdn_c = gdn_c + o(oc)
    y_lat = jnp.concatenate([ssd_out_norm(ssd_l, z_l, ssd_norm_g),
                             gdn_out_norm(gdn_l, gate_l, gdn_norm_g)], axis=-1).astype(p_lat.dtype)
    if not ctx_out:
        return y_lat, None
    y_ctx = jnp.concatenate([ssd_out_norm(ssd_c, z_c, ssd_norm_g),
                             gdn_out_norm(gdn_c, gate_c, gdn_norm_g)], axis=-1).astype(p_ctx.dtype)
    return y_lat, y_ctx

def sq_relu_mlp(h, w1, w2):
    return jnp.square(jax.nn.relu(h @ w1)) @ w2

def second_inputs(seed: int = 0) -> dict:
    key = jax.random.key(seed)
    ks = jax.random.split(key, 24)
    f32 = jnp.float32

    def nrm(k, shape, scale):
        return jax.random.normal(k, shape, f32) * scale

    def gain(k, shape):
        return 1.0 + nrm(k, shape, 0.02)

    def dt_bias(k, shape):
        dt = jnp.exp(jax.random.uniform(k, shape, f32, math.log(1e-3), math.log(1e-1)))
        return dt + jnp.log(-jnp.expm1(-dt))

    def a_log(k, shape):
        return jnp.log(jax.random.uniform(k, shape, f32, 1.0, 16.0))

    return {
        'x': nrm(ks[0], (BATCH, SEQ, D_MODEL), 1.0),
        'c': nrm(ks[1], (BATCH, D_MODEL), 1.0),
        'ctx': nrm(ks[2], (BATCH, CTX_LEN, D_MODEL), 1.0),
        'c_ctx': nrm(ks[3], (D_MODEL,), 1.0),
        'w_mod': nrm(ks[4], (DEPTH_2, D_MODEL, 6 * D_MODEL), 0.5 * D_MODEL ** -0.5),
        'b_mod': nrm(ks[5], (DEPTH_2, 6 * D_MODEL), 0.01),
        'norm1_g': gain(ks[6], (DEPTH_2, D_MODEL)),
        'w_in': nrm(ks[7], (DEPTH_2, D_MODEL, IN_DIM), D_MODEL ** -0.5),
        'ssd_conv_w': nrm(ks[8], (DEPTH_2, CONV_K, SSD_CONV_CH), CONV_K ** -0.5),
        'ssd_conv_b': nrm(ks[9], (DEPTH_2, SSD_CONV_CH), 0.01),
        'ssd_dt_bias': dt_bias(ks[10], (DEPTH_2, N_DIR, SSD_HEADS)),
        'ssd_A_log': a_log(ks[11], (DEPTH_2, N_DIR, SSD_HEADS)),
        'ssd_D': gain(ks[12], (DEPTH_2, SSD_HEADS)),
        'ssd_norm_g': gain(ks[13], (DEPTH_2, SSD_DINNER)),
        'gdn_conv_w': nrm(ks[14], (DEPTH_2, CONV_K, GDN_CONV_CH), CONV_K ** -0.5),
        'gdn_dt_bias': dt_bias(ks[15], (DEPTH_2, N_DIR, GDN_HEADS)),
        'gdn_A_log': a_log(ks[16], (DEPTH_2, N_DIR, GDN_HEADS)),
        'gdn_norm_g': gain(ks[17], (DEPTH_2, GDN_HEADDIM)),
        'w_out': nrm(ks[18], (DEPTH_2, MIX_WIDTH_2, D_MODEL), MIX_WIDTH_2 ** -0.5),
        'norm2_g': gain(ks[19], (DEPTH_2, D_MODEL)),
        'w_mlp1': nrm(ks[20], (DEPTH_2, D_MODEL, D_FF_2), D_MODEL ** -0.5),
        'w_mlp2': nrm(ks[21], (DEPTH_2, D_FF_2, D_MODEL), D_FF_2 ** -0.5),
        'final_g': gain(ks[22], (D_MODEL,)),
    }

def second_block(x, c, ctx, c_ctx, w_mod, b_mod, norm1_g, w_in, ssd_conv_w, ssd_conv_b, ssd_dt_bias,
              ssd_A_log, ssd_D, ssd_norm_g, gdn_conv_w, gdn_dt_bias, gdn_A_log, gdn_norm_g, w_out,
              norm2_g, w_mlp1, w_mlp2, final_g):
    for l in range(DEPTH_2):
        ctx_out = l < DEPTH_2 - 1
        mod_lat = (jax.nn.silu(c) @ w_mod[l] + b_mod[l])[:, None, :]
        mod_ctx = jax.nn.silu(c_ctx) @ w_mod[l] + b_mod[l]
        sh1, sc1, g1, sh2, sc2, g2 = jnp.split(mod_lat, 6, axis=-1)
        sh1c, sc1c, g1c, sh2c, sc2c, g2c = jnp.split(mod_ctx, 6, axis=-1)
        p_lat = modulate_2(rmsnorm(x, norm1_g[l]), sh1, sc1) @ w_in[l]
        p_ctx = modulate_2(rmsnorm(ctx, norm1_g[l]), sh1c, sc1c) @ w_in[l]
        y_lat, y_ctx = token_mixers(p_lat, p_ctx, ssd_conv_w[l], ssd_conv_b[l], ssd_dt_bias[l],
                                    ssd_A_log[l], ssd_D[l], ssd_norm_g[l], gdn_conv_w[l],
                                    gdn_dt_bias[l], gdn_A_log[l], gdn_norm_g[l], ctx_out)
        x = x + g1 * (y_lat @ w_out[l])
        x = x + g2 * sq_relu_mlp(modulate_2(rmsnorm(x, norm2_g[l]), sh2, sc2), w_mlp1[l], w_mlp2[l])
        if ctx_out:
            ctx = ctx + g1c * (y_ctx @ w_out[l])
            ctx = ctx + g2c * sq_relu_mlp(modulate_2(rmsnorm(ctx, norm2_g[l]), sh2c, sc2c), w_mlp1[l], w_mlp2[l])
    return rmsnorm(x, final_g)


_first_inputs = second_inputs


def second_inputs(seed=0):
    import zlib

    import numpy as np

    out = dict(_first_inputs(seed))
    spreads = {}
    factors = {'ctx': 6.154,
     'c_ctx': 8.0,
     'b_mod': 3.194,
     'norm1_g': 7.286,
     'ssd_conv_b': 64.0,
     'ssd_D': 64.0,
     'ssd_norm_g': 64.0,
     'gdn_norm_g': 21.57,
     'norm2_g': 17.724,
     'final_g': 8.01}
    for name, (base, spread) in spreads.items():
        noise = np.random.default_rng([zlib.crc32(name.encode()), seed]).standard_normal(out[name].shape)
        drawn = base * np.exp(spread * noise) if base else spread * noise
        out[name] = __import__('jax').numpy.asarray(drawn.astype(out[name].dtype))
    for name, factor in factors.items():
        out[name] = (out[name] * factor).astype(out[name].dtype)
    return out


_narrow_inputs = second_inputs


def second_inputs(seed=0):

    out = dict(_narrow_inputs(seed))
    wider = {'ssd_D': 12.0, 'ssd_norm_g': 5.6, 'gdn_norm_g': 3.3, 'final_g': 3.17}
    for name, times in wider.items():
        mean = out[name].mean()
        out[name] = (mean + times * (out[name] - mean)).astype(out[name].dtype)
    return out


def setup_inputs(seed=0):
    out = dict(first_inputs(seed))
    for name, value in second_inputs(seed + 1).items():
        if name != "x":
            out[name + "_2"] = value
    return out


def reference(
    x, c, positions, ada_w, ada_b, ffn1_norm, ffn1_w_gate, ffn1_w_up, ffn1_w_down, mix_norm,
    w_in, pool_w, pool_scale, q_a_norm, w_q_b, kv_a_norm, w_kv_b, w_out, ffn2_norm, ffn2_w_gate,
    ffn2_w_up, ffn2_w_down, final_norm, c_2, ctx_2, c_ctx_2, w_mod_2, b_mod_2, norm1_g_2,
    w_in_2, ssd_conv_w_2, ssd_conv_b_2, ssd_dt_bias_2, ssd_A_log_2, ssd_D_2, ssd_norm_g_2,
    gdn_conv_w_2, gdn_dt_bias_2, gdn_A_log_2, gdn_norm_g_2, w_out_2, norm2_g_2, w_mlp1_2,
    w_mlp2_2, final_g_2,
):
    x = first_block(
        x, c, positions, ada_w, ada_b, ffn1_norm, ffn1_w_gate, ffn1_w_up, ffn1_w_down, mix_norm,
        w_in, pool_w, pool_scale, q_a_norm, w_q_b, kv_a_norm, w_kv_b, w_out, ffn2_norm,
        ffn2_w_gate, ffn2_w_up, ffn2_w_down, final_norm,
    )
    return second_block(
        x, c_2, ctx_2, c_ctx_2, w_mod_2, b_mod_2, norm1_g_2, w_in_2, ssd_conv_w_2, ssd_conv_b_2,
        ssd_dt_bias_2, ssd_A_log_2, ssd_D_2, ssd_norm_g_2, gdn_conv_w_2, gdn_dt_bias_2,
        gdn_A_log_2, gdn_norm_g_2, w_out_2, norm2_g_2, w_mlp1_2, w_mlp2_2, final_g_2,
    )


_drawn_inputs = setup_inputs


def setup_inputs(seed=0):
    import zlib

    import numpy as np

    out = dict(_drawn_inputs(seed))
    spreads = {}
    factors = {'q_a_norm': 8.0, 'kv_a_norm': 4.805, 'ssd_D_2': 25.635}
    for name, (base, spread) in spreads.items():
        noise = np.random.default_rng([zlib.crc32(name.encode()), seed]).standard_normal(out[name].shape)
        drawn = base * np.exp(spread * noise) if base else spread * noise
        out[name] = __import__('jax').numpy.asarray(drawn.astype(out[name].dtype))
    for name, factor in factors.items():
        out[name] = (out[name] * factor).astype(out[name].dtype)
    return out
```

```python
from contextlib import ExitStack

import numpy as np

import concourse.bass as bass
from concourse import mybir

F32 = mybir.dt.float32
F32R = mybir.dt.float32r
I32 = mybir.dt.int32
ALU = mybir.AluOpType
ACT = mybir.ActivationFunctionType
AX_X = mybir.AxisListType.X
ds = bass.ds

P = 128
D = 1024
KD = D // P
N = 512
L = 2
DFF = 2816
KF = DFF // P
HALF = KF // 2
SLOT = 16 * P
EPS = 1e-6
POOL_WINDOWS = (2, 4, 8, 16)
HEADS = 4
NOPE, ROPE, DV = 128, 64, 128
QL, KVL = 384, 256
KQ, KKV = QL // P, KVL // P
SM_SCALE = 1.0 / float(np.sqrt(NOPE + ROPE))
THETA = 10000.0
HEAD_COLS = KQ * 128 + KQ * 128 + KKV * 128 + KKV * 128
PAD = 16
NEG = -1.0e30

GU_SLOTS, DOWN_SLOTS = KF, 2 * KD
FFN_SLOTS = GU_SLOTS + DOWN_SLOTS
IN_SLOTS, POOL_SLOTS, OUT_SLOTS = 5, 1, 4
MIX_SLOTS = IN_SLOTS + POOL_SLOTS + HEADS + OUT_SLOTS
LAYER_SLOTS = 2 * FFN_SLOTS + MIX_SLOTS

CHUNKS_PER_FFN = 24
FIRST_CHUNKS = 12
N_PARAMS = 27
N_CHUNKS = 4 * N_PARAMS

CT = 256
ROW = 64
CW = 5
LAT_ROWS = N // ROW
PROW = ROW + CW - 1
PLAT = LAT_ROWS * PROW
PALL = PLAT + CT + CW - 1
NC_LAT, NC_CTX = N // P, CT // P
NC_ALL = NC_LAT + NC_CTX
SSD_H, SSD_P, SSD_N = 16, 64, 64
PAIRS = SSD_H // 2
GDN_H = 8
MIX2 = 2 * D
F2 = 4 * D
IN2_SLOTS = 2 + PAIRS + 2 * GDN_H
OUT2_SLOTS = KD
UP2_SLOTS, DOWN2_SLOTS = 16, 16
LEVELS = (1, 2, 4, 8, 16, 32)
Q64 = 64

RING = 2

VEC = {}
_at = 0
for _name, _n in (("ffn1_norm", 8 * L), ("mix_norm", 8 * L), ("ffn2_norm", 8 * L), ("pool_scale", 4 * L),
                  ("q_a_norm", 3 * L), ("kv_a_norm", 2 * L), ("final_norm", 8), ("norm1_g_2", 8), ("norm2_g_2", 8),
                  ("final_g_2", 8), ("ssd_norm_g_2", 8), ("gdn_norm_g_2", 1), ("ssd_D_2", 8), ("ssd_conv_w_2", 50),
                  ("ssd_conv_b_2", 10), ("gdn_conv_w_2", 120), ("dt_bias_2", 1), ("A_log_2", 1)):
    VEC[_name] = _at
    _at += _n
N_VEC = _at


class Names:
    pass


def build(nc, a):
    K = 1024
    base = (nc.sbuf_base + 63) // 64 * 64
    ctx = ExitStack()
    with ctx:
        def at(name, shape, dt, kb):
            return nc.alloc_sbuf_tensor_at(name, shape, dt, offset=int(base + kb * K))

        def sem(name):
            return ctx.enter_context(nc.semaphore(name))

        t = Names()
        t.raw = at("raw", [P, 2, SLOT], F32, 0)
        t.whi = at("whi", [P, 2, SLOT], F32R, 16)
        t.wlo = at("wlo", [P, 2, SLOT], F32R, 32)
        t.x = at("x", [P, KD, N], F32, 48)
        t.xhi = at("xhi", [P, KD, N], F32R, 64)
        t.xlo = at("xlo", [P, KD, N], F32R, 80)
        t.hhi = at("hhi", [P, KF, N], F32R, 96)
        t.hlo = at("hlo", [P, KF, N], F32R, 140)
        t.first = at("first", [P, FIRST_CHUNKS, KD, 256], F32, 96)
        t.ada = at("ada", [P, KD, 256], F32, 184)
        t.sg = at("sg", [P, 2, N], F32, 192)
        t.hf = at("hf", [P, N], F32, 196)
        t.sq = at("sq", [P, KD, N], F32, 112)
        t.esq = at("esq", [P, KD, N], F32, 64)
        t.nt = at("nt", [P, 4, N], F32, 136)
        t.lnv = at("lnv", [P, N], F32, 144)
        t.rstd = at("rstd", [P, N], F32, 146)
        t.upad = at("upad", [P, 4, PAD + N], F32, 96)
        t.zin = at("zin", [P, 6, N], F32, 105)
        t.win = at("win", [P, 2, PAD + N], F32, 117)
        t.dif = at("dif", [P, 4, N], F32R, 122)
        t.difl = at("difl", [P, 4, N], F32R, 130)
        t.yhi = at("yhi", [P, KD, N], F32R, 138)
        t.ylo = at("ylo", [P, KD, N], F32R, 154)
        t.cos = at("cos", [P, N], F32, 170)
        t.sin = at("sin", [P, N], F32, 172)
        t.ang = at("ang", [P, 2, N], F32, 174)
        t.posf = at("posf", [P, N], F32, 178)
        t.krr = at("krr", [P, N], F32, 180)
        t.chi = at("chi", [P, 5, N], F32R, 96)
        t.clo = at("clo", [P, 5, N], F32R, 182)
        t.qn = at("qn", [P, N], F32, 117)
        t.kn = at("kn", [P, N], F32, 119)
        t.qr = at("qr", [P, N], F32, 121)
        t.vt = at("vt", [P, 4, DV], F32, 123)
        t.rt1 = at("rt1", [P, N], F32, 125)
        t.sc = at("sc", [P, 2, N], F32, 127)
        t.pr = at("pr", [P, 2, N], F32, 131)
        t.pT = at("pT", [P, 4, P], F32, 135)
        t.msq = at("msq", [P, 5, N], F32, 64)
        t.mln = at("mln", [P, 2, N], F32, 74)
        t.mrs = at("mrs", [P, 2, N], F32, 78)
        t.modT = at("modT", [P, 8 * N_PARAMS], F32, 198)
        t.adab = at("adab", [P, 8 * N_PARAMS], F32, 199)
        t.vec = at("vec", [P, N_VEC], F32, 200)
        t.ident = at("ident", [P, P], F32, 201.25)
        t.ones = at("ones", [P, P], F32, 201.75)
        t.rot = at("rot", [P, P], F32, 202.25)
        t.dmask = at("dmask", [P, P], F32, 202.75)
        t.acc = at("acc", [P, 2, 256], F32, 203.25)
        t.cs = at("cs", [P, N_PARAMS, KD], F32, 205.25)
        t.cin = at("cin", [P, 3, KD], F32, 206.125)
        t.eps = at("eps", [P, 1], F32, 206.25)
        t.Am = at("Am", [P, KD], F32, 206.3125)
        t.gm = at("gm", [P, KD], F32, 206.375)
        t.freq = at("freq", [P, 1], F32, 206.4375)
        t.pfac = at("pfac", [P, 4, PAD], F32, 206.5)
        t.st = at("st", [P, 64], F32, 206.75)
        t.ctx = at("ctx", [P, KD, CT], F32, 128)
        t.c2hi = at("c2hi", [P, KD, CT], F32R, 96)
        t.c2lo = at("c2lo", [P, KD, CT], F32R, 104)
        t.y = at("y", [P, 16, N], F32, 152)
        t.y2hi = at("y2hi", [P, 16, N], F32R, 64)
        t.y2lo = at("y2lo", [P, 16, N], F32R, 96)
        t.rl = at("rl", [P, 2, N], F32, 128)
        t.h2 = at("h2", [P, 2, N], F32, 132)
        t.tri = at("tri", [P, 7, P], F32, 184)
        t.neg = at("neg", [P, 4, P], F32, 187.5)
        t.lev = at("lev", [P, 12, P], F32, 189.5)
        t.tm1 = at("tm1", [P, NC_ALL, 96], F32, 195.5)
        t.tm2 = at("tm2", [P, NC_ALL, 64], F32, 48)
        t.acum = at("acum", [P, 2, NC_ALL, 16], F32, 49.5)
        t.wgt = at("wgt", [P, 2, NC_ALL, 16], F32, 50.25)
        t.etot = at("etot", [P, NC_ALL, 32], F32, 51)
        t.gcum = at("gcum", [P, 2, NC_ALL, 8], F32, 51.75)
        t.egc = at("egc", [P, 2, NC_ALL, 8], F32, 52.125)
        t.kdw = at("kdw", [P, 2, NC_ALL, 8], F32, 52.5)
        t.eg = at("eg", [P, 2, NC_ALL, 16], F32, 52.875)
        t.nbeta = at("nbeta", [P, NC_ALL, 16], F32, 53.625)
        t.ahm = at("ahm", [16, 2, N], F32, 54)
        t.ghm = at("ghm", [8, 2, N + CT], F32, 58)
        t.f1 = at("f1", [P, N + CT], F32, 152)
        t.f2 = at("f2", [P, N + CT], F32, 155)
        t.fa = at("fa", [P, N + CT], F32, 158)
        t.fb = at("fb", [P, N + CT], F32, 161)
        t.fc = at("fc", [P, N + CT], F32, 164)
        t.fd = at("fd", [P, N + CT], F32, 167)
        t.xp = at("xp", [P, 2, PALL], F32, 112)
        t.cacc = at("cacc", [P, 2, PALL], F32, 118.5)
        t.bf = at("bf", [P, N + CT], F32, 125)
        t.cf = at("cf", [P, N], F32, 128)
        t.btm = at("btm", [P, NC_ALL, P], F32, 130)
        t.gt = at("gt", [P, 2, NC_LAT, P], F32, 133)
        t.xa = at("xa", [P, N + CT], F32, 137)
        t.zs = at("zs", [P, N], F32, 140)
        t.xtm = at("xtm", [P, NC_ALL, P], F32, 142)
        t.xdt = at("xdt", [P, 2, NC_LAT, P], F32, 145)
        t.cpr = at("cpr", [P, N], F32, 149)
        t.hp = at("hp", [P, 2, 5, P], F32, 168)
        t.wx = at("wx", [P, 2, NC_ALL, P], F32, 173)
        t.es = at("es", [P, N], F32, 179)
        t.ecr = at("ecr", [P, N], F32, 181)
        t.sel = at("sel", [16, 2, P], F32, 183)
        t.gq = at("gq", [P, N], F32, 125)
        t.gk = at("gk", [P, N + CT], F32, 127)
        t.gate = at("gate", [P, N], F32, 130)
        t.ktm = at("ktm", [P, NC_ALL, P], F32, 132)
        t.vtm = at("vtm", [P, NC_ALL, P], F32, 135)
        t.kk = at("kk", [P, NC_ALL, P], F32, 138)
        t.qk = at("qk", [P, NC_LAT, P], F32, 141)
        t.gv = at("gv", [P, N + CT], F32, 143)
        t.dec = at("dec", [P, NC_ALL, P], F32, 143)
        t.gsq = at("gsq", [P, 2, N + CT], F32, 146)
        t.gecr = at("gecr", [P, N], F32, 146)
        t.E = at("E", [P, NC_ALL, P], F32, 146)
        t.X = at("X", [P, NC_ALL, P], F32, 149)
        t.A = at("A", [P, NC_ALL, P], F32, 112)
        t.Xt = at("Xt", [P, NC_ALL, P], F32, 115)
        t.kdec = at("kdec", [P, NC_ALL, P], F32, 118)
        t.qkd = at("qkd", [P, NC_LAT, P], F32, 121)
        t.qdec = at("qdec", [P, N], F32, 123)
        t.sel8 = at("sel8", [8, P], F32, 204.75)
        t.w0 = at("w0", [P, NC_ALL, P], F32, 48)
        t.u0 = at("u0", [P, NC_ALL, P], F32, 54)
        t.S = at("S", [P, 2, 2, P], F32, 184)
        t.vn = at("vn", [P, 2, P], F32, 186)

        gemm = ctx.enter_context(nc.psum_tensor("gemm", [P, 4, N], F32))
        misc = ctx.enter_context(nc.psum_tensor("misc", [P, 3, N], F32))
        pmod = ctx.enter_context(nc.psum_tensor("pmod", [P, N], F32))

        raw_landed = [sem("raw_landed0"), sem("raw_landed1")]
        hi_done = sem("hi_done")
        split_done = sem("split_done")
        slot_done = sem("slot_done")
        slot_evicted = sem("slot_evicted")
        ada_landed = sem("ada_landed")
        first_landed = [sem(f"first_landed{j}") for j in range(3)]
        ada_acc = sem("ada_acc")
        mod_done = sem("mod_done")
        mod_ready = sem("mod_ready")
        init_landed = sem("init_landed")
        c_silu = sem("c_silu")
        cs_ready = sem("cs_ready")
        sq_done = sem("sq_done")
        ss_done = sem("ss_done")
        rstd_done = sem("rstd_done")
        nt_ready = sem("nt_ready")
        nhi_done = sem("nhi_done")
        xn_ready = sem("xn_ready")
        silu_done = sem("silu_done")
        hhi_done = sem("hhi_done")
        h_ready = sem("h_ready")
        pos_landed = sem("pos_landed")
        ang_ready = sem("ang_ready")
        trig_done = sem("trig_done")
        pool_in = sem("pool_in")
        rotk_done = sem("rotk_done")
        c_in = sem("c_in")
        csq_done = sem("csq_done")
        css_done = sem("css_done")
        crs_done = sem("crs_done")
        c_ready = sem("c_ready")
        q_taken = sem("q_taken")
        qr_taken = sem("qr_taken")
        kv_taken = sem("kv_taken")
        v_taken = sem("v_taken")
        rotq_done = sem("rotq_done")
        qr_ready = sem("qr_ready")
        sc_done = sem("sc_done")
        max_ready = sem("max_ready")
        exp_done = sem("exp_done")
        p_ready = sem("p_ready")
        pT_done = sem("pT_done")
        pT_taken = sem("pT_taken")
        o_done = sem("o_done")
        out_stored = sem("out_stored")

        b2_landed = sem("b2_landed")
        xf_done = sem("xf_done")
        x_saved = sem("x_saved")
        x_back = sem("x_back")
        dt_taken = sem("dt_taken")
        dt_exp = sem("dt_exp")
        f_ready = sem("f_ready")
        ft_done = sem("ft_done")
        tm_ready = sem("tm_ready")
        cum_done = sem("cum_done")
        cum_taken = sem("cum_taken")
        tot_exp = sem("tot_exp")
        prep_ready = sem("prep_ready")
        hm_done = sem("hm_done")
        hm_taken = sem("hm_taken")
        xp_ready = sem("xp_ready")
        conv_done = sem("conv_done")
        act_done = sem("act_done")
        bc_done = sem("bc_done")
        bc_taken = sem("bc_taken")
        xt_done = sem("xt_done")
        xtm_ready = sem("xtm_ready")
        xdt_ready = sem("xdt_ready")
        wx_ready = sem("wx_ready")
        st_done = sem("st_done")
        hp_ready = sem("hp_ready")
        sel_ready = sem("sel_ready")
        row_done = sem("row_done")
        seg_ready = sem("seg_ready")
        msk_ready = sem("msk_ready")
        seg_exp = sem("seg_exp")
        ecr_done = sem("ecr_done")
        es_ready = sem("es_ready")
        yc_done = sem("yc_done")
        pair_done = sem("pair_done")
        pads_ready = sem("pads_ready")
        g_sq = sem("g_sq")
        g_ss = sem("g_ss")
        g_rs = sem("g_rs")
        g_hat = sem("g_hat")
        g_kt = sem("g_kt")
        g_ktm = sem("g_ktm")
        g_vt = sem("g_vt")
        g_vtm = sem("g_vtm")
        g_kk = sem("g_kk")
        g_kkt = sem("g_kkt")
        g_kb = sem("g_kb")
        g_sel = sem("g_sel")
        g_row = sem("g_row")
        g_seg = sem("g_seg")
        g_msk = sem("g_msk")
        g_dec = sem("g_dec")
        g_A = sem("g_A")
        g_ke = sem("g_ke")
        g_At = sem("g_At")
        g_X = sem("g_X")
        g_e = sem("g_e")
        g_es = sem("g_es")
        g_xe = sem("g_xe")
        g_uw = sem("g_uw")
        g_u = sem("g_u")
        g_w = sem("g_w")
        g_p = sem("g_p")
        g_vn = sem("g_vn")
        g_sd = sem("g_sd")
        g_S = sem("g_S")
        g_o = sem("g_o")
        g_osq = sem("g_osq")
        g_oss = sem("g_oss")
        g_ors = sem("g_ors")
        head_done = sem("head_done")
        ysq_done = sem("ysq_done")
        yss_done = sem("yss_done")
        yrs_done = sem("yrs_done")
        yn_ready = sem("yn_ready")
        yhi_done = sem("yhi_done")
        y2_ready = sem("y2_ready")
        rl_done = sem("rl_done")
        h2_ready = sem("h2_ready")
        h2hi_done = sem("h2hi_done")
        h2_done = sem("h2_done")
        out_ready = sem("out_ready")

        work = [gemm[:, 3], misc[:, 0], misc[:, 1], misc[:, 2], pmod[:, :]]
        xsave = nc.dram_tensor("xsave", [P, KD, N], F32, kind="Internal").ap()
        SB = L * LAYER_SLOTS
        J0 = SB // 2
        S_OUT = SB + IN2_SLOTS
        S_MLP = S_OUT + OUT2_SLOTS
        STEPS = [[(c, b) for c in (4, 5, 0, 1, 2, 3) for b in (0, 1)],
                 [(c, b) for c in (5, 4, 3, 2, 1, 0) for b in (1, 0)]]
        ORDER = [(4, 5, 0, 1, 2, 3), (5, 4, 3, 2, 1, 0)]
        NST = len(STEPS[0])
        NLV = len(LEVELS) - 1

        def vcol(name, i=0, n=1):
            return t.vec[:, ds(VEC[name] + i, n)]

        block = ctx.enter_context(nc.Block())

        NORMS = 3
        INIT = 11

        @block.sync
        def _(sp):
            for dst, src in ((t.cin[:], a.c), (t.adab[:], a.ada_b), (t.vec[:], a.vec), (t.ident[:], a.ident),
                             (t.rot[:], a.rot), (t.dmask[:], a.dmask), (t.freq[:], a.freq),
                             (t.pfac[:], a.pfac), (t.x[:], a.x), (t.ones[:], a.ones), (t.eps[:], a.eps)):
                sp.dma_start(dst, src).then_inc(init_landed, 16)

            def load_slot(h, s, src, n):
                sp.wait_ge(split_done, s + 1)
                sp.dma_start(t.raw[:, h, 0:n], src).then_inc(raw_landed[h], 16)

            def load_chunk(c):
                sp.wait_ge(ada_acc, c)
                sp.dma_start(t.ada[:], a.ada[ds(c, 1)].rearrange("a p n -> (a p) n")
                             ).then_inc(ada_landed, 16)

            for j in range(3):
                cs = slice(4 * j, 4 * j + 4)
                sp.dma_start(t.first[:, cs].rearrange("p c k n -> p c (k n)"), a.ada[cs].rearrange("c p n -> p c n")
                             ).then_inc(first_landed[j], 16)

            def slots(w, first, n, s0, cols):
                with sp.Fori(0, n // 2) as i:
                    for h in range(2):
                        load_slot(h, s0 + 2 * i + h, w[ds(first + 2 * i + h, 1)].rearrange("a p n -> (a p) n"), cols)

            def ffn(gu, down, l, s0, chunk0):
                load_slot(0, s0, gu[ds(l * GU_SLOTS, 1)].rearrange("a p n -> (a p) n"), 16 * P)
                with sp.Fori(0, GU_SLOTS // 2 - 1) as i:
                    for h in range(2):
                        load_slot(1 - h, s0 + 2 * i + h + 1,
                                  gu[ds(l * GU_SLOTS + 2 * i + h + 1, 1)].rearrange("a p n -> (a p) n"), 16 * P)
                        load_chunk(chunk0 + 2 * i + h)
                g = GU_SLOTS - 1
                load_slot(1, s0 + g, gu[ds(l * GU_SLOTS + g, 1)].rearrange("a p n -> (a p) n"), 16 * P)
                load_chunk(chunk0 + g - 1)
                for h in range(2):
                    load_slot(h, s0 + GU_SLOTS + h, down[ds(l * DOWN_SLOTS + h, 1)].rearrange("a p n -> (a p) n"), HALF * P)
                    load_chunk(chunk0 + g + h)
                load_chunk(chunk0 + CHUNKS_PER_FFN - 1)
                slots(down, l * DOWN_SLOTS + 2, DOWN_SLOTS - 2, s0 + GU_SLOTS + 2, HALF * P)

            with sp.Fori(0, L) as l:
                s0 = l * LAYER_SLOTS
                chunk0 = FIRST_CHUNKS + 2 * CHUNKS_PER_FFN * l
                ffn(a.gu1, a.down1, l, s0, chunk0)
                s1 = s0 + FFN_SLOTS
                for j in range(IN_SLOTS):
                    load_slot(j % 2, s1 + j, a.w_in[ds(l * IN_SLOTS + j, 1)].rearrange("a p n -> (a p) n"), 16 * P)
                    if j == 1:
                        sp.wait_ge(slot_evicted, s1 + RING)
                        sp.dma_start(t.posf[:].bitcast(I32), a.pos.partition_broadcast(P)).then_inc(pos_landed, 16)
                j = IN_SLOTS
                load_slot(j % 2, s1 + j, a.pool_w[ds(l, 1)].rearrange("a p n -> (a p) n"), 4 * P)
                slots(a.head_w, l * HEADS, HEADS, s1 + j + 1, HEAD_COLS)
                slots(a.w_out, l * OUT_SLOTS, OUT_SLOTS, s1 + j + 1 + HEADS, 16 * P)
                ffn(a.gu2, a.down2, l, s1 + MIX_SLOTS, chunk0 + CHUNKS_PER_FFN)

            row = lambda w, i: w[ds(i, 1)].rearrange("a p n -> (a p) n")
            for j in range(2):
                load_slot(j, SB + j, row(a.w_in2, j), 16 * P)
            sp.wait_ge(slot_evicted, SB + RING)
            sp.wait_ge(ada_acc, N_CHUNKS)
            for dst, src in ((t.ctx[:], a.ctx), (t.tri[:], a.tri), (t.neg[:], a.neg), (t.lev[:], a.lev)):
                sp.dma_start(dst, src).then_inc(b2_landed, 16)
            sp.wait_ge(xn_ready, 7 * KD)
            sp.dma_start(xsave, t.x[:]).then_inc(x_saved, 16)
            slots(a.w_in2, 2, IN2_SLOTS - 2, SB + 2, 16 * P)
            for j in range(2):
                load_slot(j, S_OUT + j, row(a.w_out2, j), 16 * P)
            sp.wait_ge(head_done, GDN_H)
            sp.wait_ge(x_saved, 16)
            sp.dma_start(t.x[:], xsave).then_inc(x_back, 16)
            slots(a.w_out2, 2, OUT2_SLOTS - 2, S_OUT + 2, 16 * P)
            for half in range(2):
                slots(a.up2, half * 8, 8, S_MLP + half * 16, 16 * P)
                slots(a.down2b, half * 8, 8, S_MLP + half * 16 + 8, 16 * P)
            sp.wait_ge(out_ready, KD)
            sp.dma_start(a.out, t.x[:]).then_inc(out_stored, 16)
            sp.wait_ge(out_stored, 16)

        @block.gpsimd
        def _(pool):
            def bc(ap, shape):
                return ap.to_broadcast(shape)

            with pool.Fori(0, PAIRS // 2) as i:
                for g in range(2):
                    u, k = 2 * i + g, 4 * g + i
                    pool.wait_ge(xtm_ready, u + 1)
                    pool.wait_ge(prep_ready, 2)
                    for d in range(2):
                        for e in range(2):
                            w = t.wgt[:, d, :, ds(2 * k + e, 1)]
                            ins = pool.tensor_tensor(t.wx[:, d, :, 64 * e:64 * e + 64], t.xtm[:, :, 64 * e:64 * e + 64],
                                                     bc(w, [P, NC_ALL, 64]), ALU.mult)
                    ins.then_inc(wx_ready, 1)
                    for r in range(4):
                        v = 4 * u + r
                        pool.wait_ge(seg_ready, v + 1)
                        es = t.es[:].rearrange("p (c n) -> p c n", c=NC_LAT)
                        pool.tensor_tensor(es, es, t.neg[:, r % 2:r % 2 + 1].to_broadcast([P, NC_LAT, P]),
                                           ALU.add).then_inc(msk_ready, 1)
            with pool.Fori(0, GDN_H) as hd:
                for d in range(2):
                    v = 2 * hd + d
                    pool.wait_ge(g_kkt, hd + 1)
                    if d == 1:
                        pool.wait_ge(g_w, v)
                    beta = t.tm1[:, :, ds(64 + 8 * d + hd, 1)]
                    pool.tensor_tensor(t.A[:], t.kk[:], bc(beta, [P, NC_ALL, P]), ALU.mult).then_inc(g_kb, 1)
                    pool.wait_ge(g_seg, v + 1)
                    pool.tensor_tensor(t.dec[:], t.dec[:], t.neg[:, 2 + d:3 + d].to_broadcast([P, NC_ALL, P]),
                                       ALU.add).then_inc(g_msk, 1)
                    pool.wait_ge(g_kb, v + 1)
                    pool.tensor_tensor((t.kdec, t.kk)[d][:], t.ktm[:], bc(t.kdw[:, d, :, ds(hd, 1)], [P, NC_ALL, P]), ALU.mult)
                    pool.wait_ge(g_A, v + 1)
                    pool.tensor_tensor(t.dec[:], t.ktm[:], bc(t.egc[:, d, :, ds(hd, 1)], [P, NC_ALL, P]),
                                       ALU.mult).then_inc(g_ke, 1)

        @block.scalar
        def _(act):
            act.wait_ge(init_landed, 16 * INIT)
            act.activation(t.cin[:], t.cin[:], ACT.Silu).then_inc(c_silu, 1)

            def hi(h, s, j):
                act.wait_ge(raw_landed[h], 16 * j + 16)
                act.wait_ge(slot_done, s + 1)
                act.activation(t.whi[:, h], t.raw[:, h], ACT.Copy).then_inc(hi_done, 1)

            def norm(n, xs, tokens, shift, s_before, mods, m=None, hi_dst=None, pre=None,
                     early=False):
                m = n if m is None else m
                hi_dst = t.xhi if hi_dst is None else hi_dst
                act.preload_act_table_set("natural_log_exp_and_others")
                act.wait_ge(mod_ready, mods)
                act.wait_ge(slot_evicted, s_before + RING)
                if pre is not None:
                    act.wait_ge(*pre)
                for k in (KD - 1,) if early else range(KD):
                    sq = t.esq if early else t.sq
                    act.activation(sq[:, k, 0:tokens], xs[:, k, 0:tokens], ACT.Square).then_inc(sq_done, 1)
                act.wait_ge(ss_done, n + 1)
                act.activation(t.lnv[:, 0:tokens], misc[:, 0, 0:tokens], ACT.Ln, bias=t.eps[:, 0:1], scale=1.0 / D)
                act.drain()
                act.activation(t.rstd[:, 0:tokens], t.lnv[:, 0:tokens], ACT.Exp, scale=-0.5).then_inc(rstd_done, 1)
                if shift is None:
                    return
                for k in range(KD):
                    act.wait_ge(nt_ready, m * KD + k + 1)
                    act.activation(hi_dst[:, k, 0:tokens], t.nt[:, k % 4, 0:tokens], ACT.Identity,
                                   bias=shift(k)).then_inc(nhi_done, 1)

            def ffn(n, param, s0, j0, f0, mods, early):
                norm(n, t.x, N, lambda k: t.modT[:, ds(param * KD + k, 1)], s0, mods, early=early)
                act.preload_act_table(ACT.Silu)
                with act.Fori(0, GU_SLOTS // 2) as i:
                    for h in range(2):
                        s = s0 + 2 * i + h
                        hi(1 - h, s + 1, j0 + i + h)
                        act.wait_ge(slot_done, s + RING + 1)
                        act.activation(t.sg[:, h], gemm[:, 2 * h], ACT.Silu).then_inc(silu_done, 1)
                        act.wait_ge(slot_evicted, s + RING + 1)
                        act.activation(t.hhi[:, ds(2 * i + h, 1)].rearrange("p a n -> p (a n)"), t.hf[:],
                                       ACT.Copy).then_inc(hhi_done, 1)

                def down(i, first):
                    for u in range(4):
                        s = s0 + GU_SLOTS + 4 * i + u
                        hi((u + 1) % 2, s + 1, j0 + GU_SLOTS // 2 + 2 * i + (u + 1) // 2)
                        if u == 2 or (u == 0 and not first):
                            act.wait_ge(slot_evicted, s + RING)
                            m = 2 * i - 1 + u // 2
                            act.activation(t.esq[:, 1 - u // 2], t.x[:, ds(m, 1)].rearrange("p a n -> p (a n)"),
                                           ACT.Square).then_inc(sq_done, 1)

                down(0, True)
                with act.Fori(1, KD // 2) as i:
                    down(i, False)

            for k in range(KD - 1):
                act.activation(t.esq[:, k], t.x[:, k], ACT.Square).then_inc(sq_done, 1)
            hi(0, 0, 0)
            with act.Fori(0, L) as l:
                s0 = l * LAYER_SLOTS
                j0 = l * (LAYER_SLOTS // 2)
                ffn(NORMS * l, 9 * l, s0, j0, 2 * l, 2 * l + 1, True)
                s1, j1 = s0 + FFN_SLOTS, j0 + FFN_SLOTS // 2
                norm(NORMS * l + 1, t.x, N, lambda k: t.modT[:, ds((9 * l + 3) * KD + k, 1)], s1, 2 * l + 2, early=True)
                for j in range(IN_SLOTS + POOL_SLOTS):
                    hi((j + 1) % 2, s1 + j + 1, j1 + (j + 1) // 2)
                    if j == 1:
                        act.wait_ge(ang_ready, 2 * l + 1)
                        act.activation(t.sin[:], t.ang[:, 0], ACT.Sin).then_inc(trig_done, 1)
                        act.wait_ge(ang_ready, 2 * l + 2)
                        act.activation(t.cos[:], t.ang[:, 1], ACT.Sin).then_inc(trig_done, 1)
                act.wait_ge(c_in, l + 1)
                act.activation(t.msq[:], t.zin[:, 0:5], ACT.Square).then_inc(csq_done, 1)
                act.wait_ge(css_done, l + 1)
                act.activation(t.mln[:, 0], misc[:, 0], ACT.Ln, bias=t.eps[:, 0:1], scale=1.0 / QL)
                act.activation(t.mln[:, 1], misc[:, 1], ACT.Ln, bias=t.eps[:, 0:1], scale=1.0 / KVL)
                act.drain()
                act.activation(t.mrs[:], t.mln[:], ACT.Exp, scale=-0.5).then_inc(crs_done, 1)
                s2, j2 = s1 + IN_SLOTS + POOL_SLOTS, j1 + (IN_SLOTS + POOL_SLOTS) // 2
                with act.Fori(0, HEADS // 2) as i:
                    for h in range(2):
                        s, hd = s2 + 2 * i + h, l * HEADS + 2 * i + h
                        hi(1 - h, s + 1, j2 + i + h)
                        act.wait_ge(slot_done, s + RING + 1)
                        act.activation(t.qn[:], gemm[:, 2 * h], ACT.Copy).then_inc(q_taken, 1)
                        act.activation(t.kn[:], misc[:, 0], ACT.Copy).then_inc(kv_taken, 1)
                        for q in range(4):
                            keys = P * (q + 1)
                            u = hd * 4 + q
                            act.wait_ge(max_ready, u + 1)
                            act.activation(t.pr[:, q % 2, 0:keys], t.sc[:, q % 2, 0:keys], ACT.Exp,
                                           bias=t.st[:, 4 * q + 1:4 * q + 2], scale=SM_SCALE,
                                           accum_out=t.st[:, 4 * q + 2:4 * q + 3]).then_inc(exp_done, 1)
                            act.wait_ge(pT_done, u + 1)
                            act.activation(t.pT[:, 0:q + 1], gemm[:, 2 * h, 0:keys].rearrange("p (a b) -> p a b", b=P),
                                           ACT.Copy).then_inc(pT_taken, 1)
                s3, j3 = s2 + HEADS, j2 + HEADS // 2
                with act.Fori(0, OUT_SLOTS // 2) as i:
                    for h in range(2):
                        hi(1 - h, s3 + 2 * i + h + 1, j3 + i + h)
                s4, j4 = s3 + OUT_SLOTS, j3 + OUT_SLOTS // 2
                ffn(NORMS * l + 2, 9 * l + 6, s4, j4, 2 * l + 1, 2 * l + 2, False)

            norm(6, t.x, N, None, SB, 2 * L + 1, early=True)
            norm(7, t.x, N, lambda k: t.modT[:, 18 * KD + k:18 * KD + k + 1], SB, 2 * L + 1, m=6, pre=(xf_done, KD))
            act.wait_ge(b2_landed, 16 * 4)
            norm(8, t.ctx, CT, lambda k: t.modT[:, 24 * KD + k:24 * KD + k + 1], SB, 2 * L + 1, m=7,
                 hi_dst=t.c2hi, pre=(xn_ready, 7 * KD))

            def rows(v, w):
                return v.rearrange("p (r w) -> p r w", r=LAT_ROWS)[:, :, w]

            def pad_lat(b, src):
                return act.activation(rows(t.xp[:, b, 0:PLAT], slice(2, 2 + ROW)), src.rearrange("p (r w) -> p r w", w=ROW), ACT.Copy)

            def pad_ctx(b, src):
                return act.activation(t.xp[:, b, PLAT + 2:PLAT + 2 + CT], src, ACT.Copy)

            def silu(b, cv, dst, bias, ctx_too):
                act.wait_ge(conv_done, cv + 1)
                kw = {"bias": bias} if bias is not None else {}
                ins = act.activation(dst[:, 0:N].rearrange("p (r w) -> p r w", w=ROW),
                                     rows(t.cacc[:, b, 0:PLAT], slice(0, ROW)), ACT.Silu, **kw)
                if ctx_too:
                    ins = act.activation(dst[:, N:N + CT], t.cacc[:, b, PLAT:PLAT + CT], ACT.Silu, **kw)
                ins.then_inc(act_done, 1)

            act.preload_act_table(ACT.Silu)
            hi(1, SB + 1, J0)
            act.wait_ge(slot_done, SB + RING + 1)
            act.wait_ge(pads_ready, 1)
            pad_lat(0, gemm[:, 0])
            pad_ctx(0, gemm[:, 2, 0:CT]).then_inc(xp_ready, 1)
            pad_lat(1, gemm[:, 1])
            pad_ctx(1, gemm[:, 2, CT:2 * CT]).then_inc(xp_ready, 1)
            silu(0, 0, t.bf, vcol("ssd_conv_b_2", 8), True)
            silu(1, 1, t.cf, vcol("ssd_conv_b_2", 9), False)
            hi(0, SB + 2, J0 + 1)
            act.wait_ge(slot_done, SB + RING + 2)
            act.activation(t.f1[64:96, 0:N], gemm[64:96, 0], ACT.Sigmoid)
            act.activation(t.f1[64:96, N:N + CT], gemm[64:96, 2, 0:CT], ACT.Sigmoid).then_inc(dt_exp, 1)
            act.preload_act_table(ACT.Exp)
            act.wait_ge(dt_taken, 1)
            act.activation(t.fb[0:64], t.fb[0:64], ACT.Exp).then_inc(dt_exp, 1)
            act.activation(t.st[:, 0:1], vcol("A_log_2"), ACT.Exp).then_inc(dt_exp, 1)
            act.wait_ge(bc_done, 1)
            act.activation(t.btm[:, 0:4], work[0].rearrange("p (c n) -> p c n", n=P), ACT.Copy)
            act.activation(t.btm[:, 4:6], work[1][:, 0:CT].rearrange("p (c n) -> p c n", n=P), ACT.Copy)
            act.activation(t.gt[:, 0], work[2].rearrange("p (c n) -> p c n", n=P), ACT.Copy)
            act.activation(t.gt[:, 1], work[3].rearrange("p (c n) -> p c n", n=P), ACT.Copy).then_inc(bc_taken, 1)
            act.wait_ge(cum_taken, 1)
            act.wait_ge(x_saved, 16)
            act.activation(t.wgt[:], t.wgt[:], ACT.Exp)
            act.activation(t.etot[:], t.etot[:], ACT.Exp)
            act.activation(t.egc[:], t.gcum[:], ACT.Exp)
            act.activation(t.kdw[:], t.kdw[:], ACT.Exp)
            act.activation(t.eg[:], t.eg[:], ACT.Exp).then_inc(tot_exp, 1)
            for d in range(2):
                act.wait_ge(hm_done, d + 1)
                act.activation(t.ahm[:, d], work[0][0:16, :], ACT.Copy)
                act.activation(t.ghm[:, d, 0:N], work[1][0:8, :], ACT.Copy)
                act.activation(t.ghm[:, d, N:N + CT], work[2][0:8, 0:CT], ACT.Copy).then_inc(hm_taken, 1)

            with act.Fori(0, PAIRS // 2) as i:
                for g in range(2):
                    u, k = 2 * i + g, 4 * g + i
                    s = SB + 2 + u
                    hi(1 - g, s + 1, J0 + 1 + i + g)
                    act.wait_ge(slot_done, s + RING + 1)
                    act.wait_ge(pair_done, u + 1)
                    act.activation(t.zs[:], gemm[:, 1], ACT.Silu)
                    pad_lat(g, gemm[:, 0])
                    pad_ctx(g, gemm[:, 2, 0:CT]).then_inc(xp_ready, 1)
                    silu(g, 2 + u, t.xa, vcol("ssd_conv_b_2", k), True)
                    act.wait_ge(xt_done, u + 1)
                    act.activation(t.xtm[:, 0:4], work[0].rearrange("p (c n) -> p c n", n=P), ACT.Copy)
                    act.activation(t.xtm[:, 4:6], work[1][:, 0:CT].rearrange("p (c n) -> p c n", n=P), ACT.Copy
                                   ).then_inc(xtm_ready, 1)
                    for r in range(4):
                        v = 4 * u + r
                        act.wait_ge(yc_done, v + 1)
                        act.wait_ge(seg_ready, v + 1)
                        act.activation(t.ecr[64 * g:64 * g + 64], work[2 + r % 2][64 * g:64 * g + 64], ACT.Exp).then_inc(ecr_done, 1)
                        act.wait_ge(msk_ready, v + 1)
                        act.activation(t.es[:], t.es[:], ACT.Exp).then_inc(seg_exp, 1)

            with act.Fori(0, GDN_H) as hd:
                s = SB + 2 + PAIRS + 2 * hd
                j = J0 + 1 + PAIRS // 2 + hd
                hi(1, s + 1, j)
                act.wait_ge(slot_done, s + RING + 1)
                act.wait_ge(pads_ready, 2 + hd)
                pad_lat(0, gemm[:, 0])
                pad_ctx(0, gemm[:, 2, 0:CT]).then_inc(xp_ready, 1)
                pad_lat(1, gemm[:, 1]).then_inc(xp_ready, 1)
                cv = 2 + PAIRS + 3 * hd
                act.preload_act_table(ACT.Silu)
                silu(0, cv, t.gk, None, True)
                silu(1, cv + 1, t.gq, None, False)
                hi(0, s + 2, j + 1)
                act.wait_ge(slot_done, s + RING + 2)
                act.activation(t.gate[:], gemm[:, 1], ACT.Silu)
                pad_lat(0, gemm[:, 0])
                pad_ctx(0, gemm[:, 2, 0:CT]).then_inc(xp_ready, 1)
                silu(0, cv + 2, t.gv, None, True)
                act.drain()
                act.activation(t.gsq[:, 0, 0:N], t.gq[:], ACT.Square)
                act.activation(t.gsq[:, 1], t.gk[:], ACT.Square).then_inc(g_sq, 1)
                act.preload_act_table_set("natural_log_exp_and_others")
                act.wait_ge(g_ss, hd + 1)
                act.activation(t.gsq[:, 0, 0:N], work[0], ACT.Ln, bias=t.eps[:, 0:1])
                act.activation(t.gsq[:, 1, 0:N], work[1], ACT.Ln, bias=t.eps[:, 0:1])
                act.activation(t.gsq[:, 1, N:N + CT], work[2][:, 0:CT], ACT.Ln, bias=t.eps[:, 0:1])
                act.drain()
                act.activation(t.gsq[:, 0, 0:N], t.gsq[:, 0, 0:N], ACT.Exp, scale=-0.5)
                act.activation(t.gsq[:, 1], t.gsq[:, 1], ACT.Exp, scale=-0.5).then_inc(g_rs, 1)
                act.wait_ge(g_vt, hd + 1)
                act.activation(t.vtm[:, 0:4], work[2].rearrange("p (c n) -> p c n", n=P), ACT.Copy)
                act.activation(t.vtm[:, 4:6], work[3][:, 0:CT].rearrange("p (c n) -> p c n", n=P), ACT.Copy).then_inc(g_vtm, 1)
                act.wait_ge(g_kt, hd + 1)
                act.activation(t.ktm[:, 0:4], work[0].rearrange("p (c n) -> p c n", n=P), ACT.Copy)
                act.activation(t.ktm[:, 4:6], work[1][:, 0:CT].rearrange("p (c n) -> p c n", n=P), ACT.Copy).then_inc(g_ktm, 1)
                act.wait_ge(g_kk, hd + 1)
                act.activation(t.kk[:, 0:4], work[2].rearrange("p (c n) -> p c n", n=P), ACT.Copy)
                act.activation(t.kk[:, 4:6], work[3][:, 0:CT].rearrange("p (c n) -> p c n", n=P), ACT.Copy)
                act.activation(t.qk[:], work[4].rearrange("p (c n) -> p c n", n=P), ACT.Copy).then_inc(g_kkt, 1)
                for d in range(2):
                    v = 2 * hd + d
                    act.wait_ge(g_seg, v + 1)
                    act.activation(t.gecr[:], work[0], ACT.Exp).then_inc(ecr_done, 1)
                    act.wait_ge(g_msk, v + 1)
                    act.activation(t.dec[:], t.dec[:], ACT.Exp).then_inc(g_dec, 1)
                    act.wait_ge(g_uw, v + 1)
                    for b in range(2):
                        ins = act.activation((t.w0, t.X)[d][:, 3 * b:3 * b + 3],
                                             work[2 + b][:, 0:3 * P].rearrange("p (c n) -> p c n", n=P), ACT.Copy)
                    ins.then_inc(g_w, 1)
                act.wait_ge(g_o, hd + 1)
                act.activation(t.E[:, 0:4].rearrange("p c n -> p (c n)"), work[4], ACT.Square).then_inc(g_osq, 1)
                act.wait_ge(g_oss, hd + 1)
                act.activation(t.X[:, 0:4].rearrange("p c n -> p (c n)"), work[0], ACT.Ln, bias=t.eps[:, 0:1], scale=1.0 / P)
                act.drain()
                act.activation(t.E[:, 0:4], t.X[:, 0:4], ACT.Exp, scale=-0.5).then_inc(g_ors, 1)

            act.wait_ge(head_done, GDN_H)
            for k in range(8):
                act.activation(t.sq[:, k], t.y[:, k], ACT.Square).then_inc(ysq_done, 1)
            act.wait_ge(yss_done, 1)
            for g in range(2):
                act.activation(t.nt[:, g], work[g], ACT.Ln, bias=t.eps[:, 0:1], scale=2.0 / D)
            act.drain()
            act.activation(t.nt[:, 2:4], t.nt[:, 0:2], ACT.Exp, scale=-0.5).then_inc(yrs_done, 1)
            for k in range(16):
                if k < 8:
                    act.wait_ge(yn_ready, k + 1)
                act.activation(t.y2hi[:, k], t.y[:, k], ACT.Copy).then_inc(yhi_done, 1)
            with act.Fori(0, OUT2_SLOTS // 2) as i:
                for h in range(2):
                    hi(1 - h, S_OUT + 2 * i + h + 1, S_OUT // 2 + i + h)
            norm(9, t.x, N, lambda k: t.modT[:, 21 * KD + k:21 * KD + k + 1], S_MLP, 2 * L + 1, m=8)
            for half in range(2):
                s0, j0 = S_MLP + 16 * half, (S_MLP + 16 * half) // 2
                with act.Fori(0, 4) as i:
                    for h in range(2):
                        s = s0 + 2 * i + h
                        hi(1 - h, s + 1, j0 + i + h)
                        act.wait_ge(slot_done, s + RING + 1)
                        act.activation(t.rl[:], gemm[:, 2 * h:2 * h + 2], ACT.Relu).then_inc(rl_done, 1)
                        act.wait_ge(h2_ready, 8 * half + 2 * i + h + 1)
                        act.activation(t.hhi[:, ds(4 * i + 2 * h, 2)], t.h2[:], ACT.Copy).then_inc(h2hi_done, 1)
                for n in range(7 if half else 8):
                    hi((n + 1) % 2, s0 + 8 + n + 1, j0 + 4 + (n + 1) // 2)
            norm(10, t.x, N, None, S_MLP + 32, 2 * L + 1)

        @block.vector
        def _(dve):
            dve.wait_ge(init_landed, 16 * INIT)
            dve.memset(t.raw[:], 0.0).then_inc(split_done, RING)
            dve.drain().then_inc(slot_evicted, RING)
            dve.wait_ge(c_silu, 1)
            for lo, n, j in ((0, 18, 0), (18, 6, 1), (24, 3, 2)):
                dve.tensor_copy(t.cs[:, lo:lo + n], t.cin[:, j:j + 1].to_broadcast([P, n, KD]))
            dve.drain().then_inc(cs_ready, 1)

            def chunk(c, par, b):
                cond = t.cs[:, ds(par, 1)]
                dve.wait_ge(ada_landed, 16 * (c - FIRST_CHUNKS) + 16)
                dve.wait_ge(mod_done, c + 1)
                for k in range(KD):
                    sc = cond[:, :, k:k + 1].rearrange("p a n -> p (a n)")
                    if k == 0:
                        ins = dve.tensor_scalar(t.acc[:, b], t.ada[:, k], sc, None, ALU.mult)
                    else:
                        dve.drain()
                        ins = dve.scalar_tensor_tensor(t.acc[:, b], t.ada[:, k], sc, t.acc[:, b], ALU.mult, ALU.add)
                ins.then_inc(ada_acc, 1)

            def flush(first, cols, chunks):
                dve.wait_ge(mod_done, chunks + RING)
                dve.tensor_tensor(t.modT[:, ds(first, cols)], pmod[:, ds(first, cols)], t.adab[:, ds(first, cols)],
                                  ALU.add).then_inc(mod_ready, 1)

            def lo(h, s):
                dve.wait_ge(hi_done, s + 1)
                dve.tensor_tensor(t.wlo[:, h], t.raw[:, h], t.whi[:, h].bitcast(F32),
                                  ALU.subtract).then_inc(split_done, 1)

            def norm(n, xs, tokens, gain, scale, shift, m=None, dst=None):
                m = n if m is None else m
                hi_dst, lo_dst = dst or (t.xhi, t.xlo)
                dve.drain()
                dve.scalar_tensor_tensor(t.Am[:], scale, 1.0, gain, ALU.add, ALU.mult)
                dve.drain()
                dve.wait_ge(rstd_done, n + 1)

                def low(k):
                    dve.wait_ge(nhi_done, m * KD + k + 1)
                    dve.scalar_tensor_tensor(lo_dst[:, k, 0:tokens], t.nt[:, k % 4, 0:tokens], shift(k),
                                             hi_dst[:, k, 0:tokens].bitcast(F32), ALU.add, ALU.subtract
                                             ).then_inc(xn_ready, 1)

                for k in range(KD):
                    if k >= 2:
                        low(k - 2)
                    dve.scalar_tensor_tensor(t.nt[:, k % 4, 0:tokens], xs[:, k, 0:tokens], t.Am[:, k:k + 1],
                                             t.rstd[:, 0:tokens], ALU.mult, ALU.mult).then_inc(nt_ready, 1)
                low(KD - 2)
                low(KD - 1)

            def ffn(n, param, gain, s0, chunk0, par0, f0):
                norm(n, t.x, N, gain, t.modT[:, ds((param + 1) * KD, KD)],
                     lambda k: t.modT[:, ds(param * KD + k, 1)])
                dve.tensor_scalar(t.gm[:], t.modT[:, ds((param + 2) * KD, KD)], 0.5, None, ALU.mult)
                def gu(i, h, par):
                    s = s0 + 2 * i + h
                    dve.drain()
                    lo(1 - h, s + 1)
                    chunk(chunk0 + 2 * i + h, par, h)
                    dve.wait_ge(silu_done, f0 * GU_SLOTS + 2 * i + h + 1)
                    dve.tensor_tensor(t.hf[:], t.sg[:, h], gemm[:, 2 * h + 1], ALU.mult).then_inc(slot_evicted, 1)
                    dve.wait_ge(hhi_done, f0 * GU_SLOTS + 2 * i + h + 1)
                    col = ds(2 * i + h, 1)
                    dve.tensor_tensor(t.hlo[:, col].rearrange("p a n -> p (a n)"), t.hf[:],
                                      t.hhi[:, col].rearrange("p a n -> p (a n)").bitcast(F32),
                                      ALU.subtract).then_inc(h_ready, 1)

                with dve.Fori(0, GU_SLOTS // 2) as i:
                    for h in range(2):
                        gu(i, h, par0 + i // 2)

                def down(i, first):
                    for u in range(4):
                        s = s0 + GU_SLOTS + 4 * i + u
                        lo((u + 1) % 2, s + 1)
                        if first and u < 2:
                            chunk(chunk0 + GU_SLOTS + u, par0 + GU_SLOTS // 4, u)
                        if first and u == 3:
                            flush(2 * chunk0, 2 * CHUNKS_PER_FFN, chunk0 + CHUNKS_PER_FFN)
                        dve.drain()
                        dve.wait_ge(slot_done, s + RING + 1)
                        if u % 2:
                            m = ds(2 * i + u // 2, 1)
                            xm = t.x[:, m].rearrange("p a n -> p (a n)")
                            dve.scalar_tensor_tensor(xm, gemm[:, u - 1], t.gm[:, m], xm, ALU.mult, ALU.add
                                                     ).then_inc(slot_evicted, 1)
                        else:
                            dve.sem_inc(slot_evicted, 1)

                down(0, True)
                with dve.Fori(1, KD // 2) as i:
                    down(i, False)

            def split(src, hi_ap, lo_ap):
                dve.tensor_copy(hi_ap, src)
                dve.drain()
                return dve.tensor_tensor(lo_ap, src, hi_ap.bitcast(F32), ALU.subtract)

            dve.wait_ge(mod_done, FIRST_CHUNKS + RING)
            dve.tensor_tensor(t.modT[:, 0:2 * FIRST_CHUNKS], pmod[:, 0:2 * FIRST_CHUNKS], t.adab[:, 0:2 * FIRST_CHUNKS],
                              ALU.add).then_inc(mod_ready, 1)
            lo(0, 0)

            C1 = 6.28125
            C2 = float(np.float32(2 * np.pi - C1))
            C3 = float(2 * np.pi - C1 - C2)
            MAGIC = 1.5 * 2.0 ** 23

            with dve.Fori(0, L) as l:
                s0 = l * LAYER_SLOTS
                chunk0 = FIRST_CHUNKS + 2 * CHUNKS_PER_FFN * l
                par0 = 3 + 12 * l

                def gain(name, n=KD, l=l):
                    return t.vec[:, ds(VEC[name] + l * n, n)]

                ffn(NORMS * l, 9 * l, gain("ffn1_norm"), s0, chunk0, par0, 2 * l)
                s1 = s0 + FFN_SLOTS
                m1 = 9 * l + 3
                norm(NORMS * l + 1, t.x, N, gain("mix_norm"), t.modT[:, ds((m1 + 1) * KD, KD)],
                     lambda k: t.modT[:, ds(m1 * KD + k, 1)])
                def angles():
                    dve.wait_ge(pos_landed, 16 * l + 16)
                    dve.tensor_copy(t.zin[:, 0], t.posf[:].bitcast(I32))
                    dve.drain()
                    dve.tensor_scalar(t.posf[:], t.zin[:, 0], t.freq[:, 0:1], None, ALU.mult)
                    dve.drain()
                    for j, turn in ((0, 0.0), (1, 0.25)):
                        w = t.zin[:, 1 + j]
                        dve.tensor_scalar(w, t.posf[:], float(1 / (2 * np.pi)), turn, ALU.mult, ALU.add)
                        dve.drain()
                        dve.tensor_scalar(w, w, MAGIC, None, ALU.add)
                        dve.drain()
                        dve.tensor_scalar(w, w, MAGIC, None, ALU.subtract)
                        dve.drain()
                        dve.scalar_tensor_tensor(t.ang[:, j], w, -C1, t.posf[:], ALU.mult, ALU.add)
                        for c in (C2, C3):
                            dve.drain()
                            dve.scalar_tensor_tensor(t.ang[:, j], w, -c, t.ang[:, j], ALU.mult, ALU.add)
                        dve.drain()
                        dve.tensor_scalar(t.ang[:, j], t.ang[:, j], float(turn * 2 * np.pi), float(np.float32(3.1415925)), ALU.add, ALU.min)
                        dve.drain()
                        dve.tensor_scalar(t.ang[:, j], t.ang[:, j], float(np.float32(-3.1415925)), None, ALU.max).then_inc(ang_ready, 1)

                def window(g):
                    w = POOL_WINDOWS[g]
                    cur, step, b = t.upad[:, g], 1, 0
                    dve.drain()
                    while step < w:
                        nxt = t.win[:, b]
                        dve.tensor_tensor(nxt[:, PAD:], cur[:, PAD:], cur[:, PAD - step:PAD + N - step], ALU.add)
                        dve.drain()
                        cur, step, b = nxt, 2 * step, 1 - b
                    dve.tensor_tensor(cur[:, PAD:2 * PAD], cur[:, PAD:2 * PAD], t.pfac[:, g], ALU.mult)
                    dve.drain()
                    d = t.win[:, b, PAD:]
                    dve.scalar_tensor_tensor(d, cur[:, PAD:], 1.0 / w, t.upad[:, g, PAD:], ALU.mult, ALU.subtract)
                    dve.drain()
                    return split(d, t.dif[:, g], t.difl[:, g])

                dve.memset(t.upad[:, :, 0:PAD], 0.0)
                dve.memset(t.win[:, :, 0:PAD], 0.0)
                for j in range(IN_SLOTS):
                    lo((j + 1) % 2, s1 + j + 1)
                    dve.wait_ge(slot_done, s1 + j + RING + 1)
                    dst = t.upad[:, 2 * j:2 * j + 2, PAD:] if j < 2 else t.zin[:, 2 * j - 4:2 * j - 2]
                    dve.tensor_copy(dst, gemm[:, 2 * (j % 2):2 * (j % 2) + 2]).then_inc(slot_evicted, 1)
                    if j == 0:
                        angles()
                    if j == 1:
                        window(0)
                        window(1)
                    if j == 2:
                        window(2)
                    if j == 3:
                        window(3).then_inc(pool_in, 1)
                dve.drain().then_inc(c_in, 1)
                lo(0, s1 + IN_SLOTS + 1)
                sp_ = s1 + IN_SLOTS
                dve.wait_ge(slot_done, sp_ + RING + 1)
                ps = VEC["pool_scale"] + l * 4
                for g in range(4):
                    d = t.win[:, g % 2, PAD:]
                    if g < 2:
                        src = gemm[:, 2 + g]
                    else:
                        src = misc[:, g - 1]
                    dve.tensor_scalar(d, src, t.vec[:, ds(ps + g, 1)], None, ALU.mult)
                    dve.drain()
                    ins = split(d, t.yhi[:, g], t.ylo[:, g])
                ins.then_inc(slot_evicted, 1)
                dve.wait_ge(trig_done, 2 * l + 2)
                dve.wait_ge(rotk_done, l + 1)
                dve.tensor_tensor(t.krr[:], t.zin[:, 5], t.cos[:], ALU.mult)
                dve.tensor_tensor(t.win[:, 0, 0:N], misc[:, 0], t.sin[:], ALU.mult)
                dve.drain()
                dve.tensor_tensor(t.krr[:], t.krr[:], t.win[:, 0, 0:N], ALU.add).then_inc(v_taken, 1)
                dve.wait_ge(crs_done, l + 1)
                for k in range(5):
                    g = t.vec[:, ds((VEC["q_a_norm"] + l * 3 + k) if k < 3 else (VEC["kv_a_norm"] + l * 2 + k - 3), 1)]
                    d = t.win[:, k % 2, 0:N]
                    dve.scalar_tensor_tensor(d, t.zin[:, k], g, t.mrs[:, 0 if k < 3 else 1], ALU.mult, ALU.mult)
                    dve.drain()
                    ins = split(d, t.chi[:, k], t.clo[:, k])
                ins.then_inc(c_ready, 1)
                s2 = sp_ + 1
                with dve.Fori(0, HEADS // 2) as i:
                    for h in range(2):
                        s, hd = s2 + 2 * i + h, l * HEADS + 2 * i + h
                        lo(1 - h, s + 1)
                        dve.wait_ge(slot_done, s + RING + 1)
                        dve.tensor_copy(t.qr[:], gemm[:, 2 * h + 1]).then_inc(qr_taken, 1)
                        dve.tensor_copy(t.vt[:].rearrange("p a b -> p (a b)"), misc[:, 1]).then_inc(v_taken, 1)
                        dve.drain()
                        dve.wait_ge(rotq_done, hd + 1)
                        dve.tensor_tensor(t.qr[:], t.qr[:], t.cos[:], ALU.mult)
                        dve.tensor_tensor(t.rt1[:], misc[:, 2], t.sin[:], ALU.mult)
                        dve.drain()
                        dve.tensor_tensor(t.qr[:], t.qr[:], t.rt1[:], ALU.add).then_inc(qr_ready, 1)
                        for q in range(4):
                            keys, u = P * (q + 1), hd * 4 + q
                            bank = misc[:, 2 * (q % 2)]
                            smx, nmx, rsum, rinv = (t.st[:, 4 * q + r:4 * q + r + 1] for r in range(4))
                            dve.wait_ge(sc_done, u + 1)
                            if q:
                                dve.tensor_copy(t.sc[:, q % 2, 0:P * q], bank[:, 0:P * q])
                            dve.tensor_tensor(t.sc[:, q % 2, P * q:keys], bank[:, P * q:keys], t.dmask[:], ALU.add)
                            dve.drain()
                            dve.reduce_max(smx, t.sc[:, q % 2, 0:keys], AX_X)
                            dve.drain()
                            dve.tensor_scalar(nmx, smx, -SM_SCALE, None, ALU.mult).then_inc(max_ready, 1)
                            dve.wait_ge(exp_done, u + 1)
                            dve.reciprocal(rinv, rsum)
                            dve.drain()
                            dve.tensor_scalar(t.pr[:, q % 2, 0:keys], t.pr[:, q % 2, 0:keys], rinv, None,
                                              ALU.mult).then_inc(p_ready, 1)
                        dve.wait_ge(o_done, hd + 1)
                        tile = ds(4 + 2 * i + h, 1)
                        yh = t.yhi[:, tile].rearrange("p a n -> p (a n)")
                        yl = t.ylo[:, tile].rearrange("p a n -> p (a n)")
                        split(gemm[:, 2 * h + 1], yh, yl).then_inc(slot_evicted, 1)
                s3 = s2 + HEADS
                with dve.Fori(0, OUT_SLOTS // 2) as i:
                    for h in range(2):
                        s = s3 + 2 * i + h
                        lo(1 - h, s + 1)
                        dve.wait_ge(slot_done, s + RING + 1)
                        for j in range(2):
                            m = 4 * i + 2 * h + j
                            xm = t.x[:, ds(m, 1)].rearrange("p a n -> p (a n)")
                            ins = dve.scalar_tensor_tensor(xm, gemm[:, 2 * h + j], t.modT[:, ds((m1 + 2) * KD + m, 1)],
                                                           xm, ALU.mult, ALU.add)
                        ins.then_inc(slot_evicted, 1)
                s4 = s3 + OUT_SLOTS
                ffn(NORMS * l + 2, 9 * l + 6, gain("ffn2_norm"), s4, chunk0 + CHUNKS_PER_FFN, par0 + 6, 2 * l + 1)

            def plain(n, gain, done):
                dve.wait_ge(rstd_done, n + 1)
                for k in range(KD):
                    dve.scalar_tensor_tensor(t.x[:, k], t.x[:, k], vcol(gain, k), t.rstd[:], ALU.mult, ALU.mult
                                             ).then_inc(done, 1)

            def by_token(ap):
                return ap.rearrange("p (c n) -> p c n", n=P)

            plain(6, "final_norm", xf_done)
            norm(7, t.x, N, vcol("norm1_g_2", 0, KD), t.modT[:, 19 * KD:20 * KD],
                 lambda k: t.modT[:, 18 * KD + k:18 * KD + k + 1], m=6)
            dve.wait_ge(b2_landed, 16 * 4)
            norm(8, t.ctx, CT, vcol("norm1_g_2", 0, KD), t.modT[:, 25 * KD:26 * KD],
                 lambda k: t.modT[:, 24 * KD + k:24 * KD + k + 1], m=7, dst=(t.c2hi, t.c2lo))
            dve.drain()
            dve.memset(t.xp[:], 0.0).then_inc(pads_ready, 1)
            dve.drain().then_inc(pair_done, 1)
            dve.drain().then_inc(yc_done, 1)

            def conv(b, cv, w, n, take=None):
                dve.wait_ge(xp_ready, cv + 1)
                ins = dve.tensor_scalar(t.cacc[:, b, 0:n], t.xp[:, b, 0:n], w(0), None, ALU.mult)
                if take is not None:
                    ins.then_inc(slot_evicted, 1)
                for k in range(1, CW):
                    dve.drain()
                    ins = dve.scalar_tensor_tensor(t.cacc[:, b, 0:n], t.xp[:, b, k:k + n], w(k), t.cacc[:, b, 0:n],
                                                   ALU.mult, ALU.add)
                ins.then_inc(conv_done, 1)

            def taps(name, tile):
                return lambda k: vcol(name, tile * CW + k)

            NA, NL = PALL - CW + 1, PLAT - CW + 1
            lo(1, SB + 1)
            dve.wait_ge(xp_ready, 2)
            conv(0, 0, taps("ssd_conv_w_2", 8), NA, take=True)
            conv(1, 1, taps("ssd_conv_w_2", 9), NL)
            lo(0, SB + 2)
            dve.wait_ge(slot_done, SB + RING + 2)
            bias = t.vec[0:64, VEC["dt_bias_2"]:VEC["dt_bias_2"] + 1]
            dve.tensor_scalar(t.fa[0:64, 0:N], gemm[0:64, 0], bias, None, ALU.add)
            dve.tensor_scalar(t.fa[0:64, N:N + CT], gemm[0:64, 2, 0:CT], bias, None, ALU.add)
            dve.drain()
            R = slice(0, 64)
            dve.scalar_tensor_tensor(t.fb[R], t.fa[R], -1.0, t.fa[R], ALU.mult, ALU.min).then_inc(dt_taken, 1)
            dve.wait_ge(dt_exp, 3)
            dve.tensor_scalar(t.fc[R], t.fb[R], 2.0, None, ALU.add)
            dve.drain()
            dve.reciprocal(t.fd[R], t.fc[R])
            dve.drain()
            dve.tensor_tensor(t.fb[R], t.fb[R], t.fd[R], ALU.mult)
            dve.drain()
            dve.tensor_tensor(t.fc[R], t.fb[R], t.fb[R], ALU.mult)
            dve.drain()
            dve.tensor_scalar(t.fd[R], t.fc[R], 1.0 / 15, None, ALU.mult)
            for n in (13, 11, 9, 7, 5, 3):
                dve.drain()
                dve.scalar_tensor_tensor(t.fd[R], t.fd[R], 1.0 / n, t.fc[R], ALU.add, ALU.mult)
            dve.drain()
            dve.scalar_tensor_tensor(t.fd[R], t.fd[R], 1.0, t.fb[R], ALU.add, ALU.mult)
            dve.drain()
            dve.tensor_scalar(t.fd[R], t.fd[R], 2.0, None, ALU.mult)
            dve.drain()
            dve.scalar_tensor_tensor(t.f1[R], t.fa[R], 0.0, t.fd[R], ALU.max, ALU.add)
            dve.drain()
            dve.tensor_scalar(t.f2[R], t.f1[R], t.st[R, 0:1], -1.0, ALU.mult, ALU.mult).then_inc(f_ready, 1)
            dve.sem_inc(slot_evicted, 1)
            dve.wait_ge(ft_done, 1)
            dve.wait_ge(x_saved, 16)
            dve.tensor_copy(t.tm1[:, 0:3], work[0][:, 0:288].rearrange("p (c n) -> p c n", n=96))
            dve.tensor_copy(t.tm1[:, 3:6], work[1][:, 0:288].rearrange("p (c n) -> p c n", n=96))
            dve.tensor_copy(t.tm2[:], work[2][:, 0:384].rearrange("p (c n) -> p c n", n=64)).then_inc(tm_ready, 1)
            dve.wait_ge(cum_done, 1)
            v1 = work[0][:, 0:192].rearrange("p (d c h) -> p d c h", d=2, c=NC_ALL)
            dve.tensor_copy(t.acum[:], v1)
            dve.tensor_copy(t.etot[:], work[0][:, 192:384].rearrange("p (c h) -> p c h", c=NC_ALL))
            dve.tensor_copy(t.gcum[:], work[1][:, 0:96].rearrange("p (d c h) -> p d c h", d=2, c=NC_ALL))
            dve.tensor_copy(t.eg[:], work[1][:, 192:384].rearrange("p (b c h) -> p b c h", b=2, c=NC_ALL))
            dve.tensor_scalar(t.nbeta[:], t.tm1[:, :, 64:80], -1.0, None, ALU.mult)
            dve.drain()
            for d in range(2):
                dve.tensor_tensor(t.wgt[:, d], t.etot[:, :, 16 * d:16 * d + 16], t.acum[:, d], ALU.subtract)
                tot = work[1][:, 96:192].rearrange("p (c h) -> p c h", c=NC_ALL)
                ins = dve.tensor_tensor(t.kdw[:, d], tot[:, :, 8 * d:8 * d + 8], t.gcum[:, d], ALU.subtract)
            ins.then_inc(cum_taken, 1)
            dve.wait_ge(tot_exp, 1)
            for d in range(2):
                ins = dve.tensor_tensor(t.wgt[:, d], t.wgt[:, d], t.tm1[:, :, 16 * d:16 * d + 16], ALU.mult)
            ins.then_inc(prep_ready, 2)

            with dve.Fori(0, PAIRS // 2) as i:
                for g in range(2):
                    u, k = 2 * i + g, 4 * g + i
                    s = SB + 2 + u
                    G = slice(64 * g, 64 * g + 64)
                    lo(1 - g, s + 1)
                    for e in range(2):
                        dve.tensor_scalar(t.sel[:, e], t.ones[0:16], t.ident[0:16, ds(2 * k + e, 1)], None,
                                          ALU.mult).then_inc(sel_ready, 1)
                    conv(g, 2 + u, taps("ssd_conv_w_2", k), NA, take=True)
                    dve.wait_ge(xtm_ready, u + 1)
                    for d in range(2):
                        for e in range(2):
                            c = slice(64 * e, 64 * e + 64)
                            w = t.tm1[:, 0:NC_LAT, ds(16 * d + 2 * k + e, 1)]
                            ins = dve.tensor_tensor(t.xdt[:, d, :, c], t.xtm[:, 0:NC_LAT, c],
                                                    w.to_broadcast([P, NC_LAT, 64]), ALU.mult)
                    ins.then_inc(xdt_ready, 1)
                    for d in range(2):
                        dve.wait_ge(st_done, 2 * u + d + 1)
                        for n, c in enumerate(ORDER[d][0:5]):
                            add = work[0][G, P * c:P * c + P] if c < 4 else work[1][G, P * (c - 4):P * (c - 4) + P]
                            if n == 0:
                                ins = dve.tensor_copy(t.hp[G, d, 0], add)
                                continue
                            dve.drain()
                            for e in range(2):
                                q = slice(64 * e, 64 * e + 64)
                                ins = dve.scalar_tensor_tensor(t.hp[G, d, n, q], t.hp[G, d, n - 1, q],
                                                               t.etot[G, c, ds(16 * d + 2 * k + e, 1)], add[:, q],
                                                               ALU.mult, ALU.add)
                        ins.then_inc(hp_ready, 1)
                    for r in range(4):
                        e, d = r // 2, r % 2
                        v = 4 * u + r
                        dve.wait_ge(row_done, v + 1)
                        dve.wait_ge(yc_done, v + 1)
                        w = t.acum[:, d, 0:NC_LAT, ds(2 * k + e, 1)]
                        dve.tensor_tensor(by_token(t.es[:]), by_token(work[2 + r % 2]),
                                          w.to_broadcast([P, NC_LAT, P]), ALU.subtract).then_inc(seg_ready, 1)
                        dve.wait_ge(ecr_done, v + 1)
                        dve.tensor_tensor(t.cpr[G], t.cf[G], t.ecr[G], ALU.mult)
                        dve.wait_ge(seg_exp, v + 1)
                        dve.tensor_tensor(by_token(t.es[:]), by_token(t.es[:]), t.gt[:, g], ALU.mult).then_inc(es_ready, 1)
                    dve.wait_ge(yc_done, 4 * u + 4 + 1)
                    dve.scalar_tensor_tensor(t.cpr[:], t.xa[:, 0:N], vcol("ssd_D_2", k), work[4], ALU.mult, ALU.add)
                    dve.drain()
                    dve.tensor_tensor(t.y[:, ds(k, 1)].rearrange("p a n -> p (a n)"), t.cpr[:], t.zs[:], ALU.mult)
                    dve.drain().then_inc(pair_done, 1)

            with dve.Fori(0, GDN_H) as hd:
                s = SB + 2 + PAIRS + 2 * hd
                cv = 2 + PAIRS + 3 * hd
                dve.drain()
                dve.memset(t.xp[:], 0.0).then_inc(pads_ready, 1)
                lo(1, s + 1)
                dve.wait_ge(xp_ready, cv + 2)
                conv(0, cv, taps("gdn_conv_w_2", 8 + hd), NA, take=True)
                conv(1, cv + 1, taps("gdn_conv_w_2", hd), NL)
                lo(0, s + 2)
                dve.wait_ge(act_done, cv + 1)
                conv(0, cv + 2, taps("gdn_conv_w_2", 16 + hd), NA, take=True)
                dve.wait_ge(g_rs, hd + 1)
                dve.scalar_tensor_tensor(t.gq[:], t.gq[:], float(P) ** -0.5, t.gsq[:, 0, 0:N], ALU.mult, ALU.mult)
                dve.tensor_tensor(t.gk[:], t.gk[:], t.gsq[:, 1], ALU.mult).then_inc(g_hat, 1)
                for d in range(2):
                    v = 2 * hd + d
                    dve.tensor_scalar(t.sel8[:], t.ones[0:8], t.ident[0:8, ds(hd, 1)], None, ALU.mult).then_inc(g_sel, 1)
                    dve.wait_ge(g_row, v + 1)
                    gcb = t.gcum[:, d, :, ds(hd, 1)].to_broadcast([P, NC_ALL, P])
                    dve.tensor_tensor(t.dec[:, 0:4], by_token(work[0]), gcb[:, 0:4], ALU.subtract)
                    dve.tensor_tensor(t.dec[:, 4:6], by_token(work[1][:, 0:CT]), gcb[:, 4:6], ALU.subtract).then_inc(g_seg, 1)
                    dve.wait_ge(ecr_done, 4 * PAIRS + v + 1)
                    dve.tensor_tensor((t.qdec, t.gq)[d][:], t.gq[:], t.gecr[:], ALU.mult)
                    dve.wait_ge(g_dec, v + 1)
                    dve.wait_ge(g_kb, v + 1)
                    dve.tensor_tensor(t.A[:], t.A[:], t.dec[:], ALU.mult)
                    dve.tensor_tensor((t.qkd, t.qk)[d][:], t.qk[:], t.dec[:, 0:4], ALU.mult).then_inc(g_A, 1)
                    one = t.ident[:].unsqueeze(1).to_broadcast([P, NC_ALL, P])
                    lev = lambda n, c=NC_ALL: t.lev[:, n:n + 1].to_broadcast([P, c, P])
                    halves = [(slice(0, 3), by_token(work[0][:, 0:3 * P]), by_token(work[2][:, 0:3 * P])),
                              (slice(3, 6), by_token(work[1][:, 0:3 * P]), by_token(work[3][:, 0:3 * P]))]
                    dve.drain()
                    dve.tensor_tensor(t.Xt[:], t.A[:], lev(6 * (1 - d)), ALU.mult)
                    dve.drain()
                    dve.tensor_tensor(t.Xt[:], one, t.Xt[:], ALU.subtract)
                    dve.wait_ge(g_At, v + 1)
                    for b, (cs, bank, _) in enumerate(halves):
                        dve.tensor_tensor(t.X[:, cs], bank, lev(6 * d, 3), ALU.mult)
                    dve.drain()
                    for b, (cs, _, _) in enumerate(halves):
                        dve.tensor_tensor(t.X[:, cs], one[:, cs], t.X[:, cs], ALU.subtract).then_inc(g_X, 1)
                    for n in range(NLV):
                        q = 2 * (v * NLV + n)
                        for b, (cs, bank, _) in enumerate(halves):
                            dve.wait_ge(g_e, q + b + 1)
                            dve.tensor_tensor(t.E[:, cs], bank, lev(6 * d + n + 1, 3), ALU.mult).then_inc(g_es, 1)
                        for b, (cs, bank, bank2) in enumerate(halves):
                            dve.wait_ge(g_xe, q + b + 1)
                            ins = dve.tensor_tensor(t.Xt[:, cs], t.Xt[:, cs], bank, ALU.subtract)
                            if n < NLV - 1:
                                ins = dve.tensor_tensor(t.X[:, cs], t.X[:, cs], bank2, ALU.subtract)
                            ins.then_inc(g_X, 1)
                    dve.wait_ge(g_uw, v + 1)
                    beta = t.tm1[:, :, ds(64 + 8 * d + hd, 1)].to_broadcast([P, NC_ALL, P])
                    for cs, bank, _ in halves:
                        ins = dve.tensor_tensor((t.u0, t.E)[d][:, cs], bank, beta[:, cs], ALU.mult)
                    ins.then_inc(g_u, 1)
                dve.drain()
                for n in range(NST):
                    for d in range(2):
                        c, b = STEPS[d][n]
                        H = slice(Q64 * b, Q64 * b + Q64)
                        u = (t.u0, t.E)[d]
                        if n == 0:
                            dve.tensor_copy(t.vn[H, d], u[H, c]).then_inc(g_vn, 1)
                        else:
                            dve.wait_ge(g_p, 2 * (NST - 1) * hd + 2 * (n - 1) + d + 1)
                            dve.scalar_tensor_tensor(t.vn[H, d], work[d][H, 0:P], t.nbeta[H, c, ds(8 * d + hd, 1)], u[H, c],
                                                     ALU.mult, ALU.add).then_inc(g_vn, 1)
                    if n == NST - 1:
                        continue
                    for d in range(2):
                        c, b = STEPS[d][n]
                        dve.wait_ge(g_sd, 2 * (NST - 1) * hd + 2 * n + d + 1)
                        if n == 0:
                            dve.tensor_copy(t.S[:, d, 0], work[2 + d][:, 0:P]).then_inc(g_S, 1)
                        else:
                            dve.scalar_tensor_tensor(t.S[:, d, n % 2], t.S[:, d, 1 - n % 2], t.eg[:, b, c, ds(8 * d + hd, 1)],
                                                     work[2 + d][:, 0:P], ALU.mult, ALU.add).then_inc(g_S, 1)
                dve.wait_ge(g_ors, hd + 1)
                dve.scalar_tensor_tensor(t.qdec[:], work[4], vcol("gdn_norm_g_2"), t.E[:, 0:4].rearrange("p c n -> p (c n)"),
                                         ALU.mult, ALU.mult)
                dve.drain()
                dve.tensor_tensor(t.y[:, ds(8 + hd, 1)].rearrange("p a n -> p (a n)"), t.qdec[:], t.gate[:], ALU.mult
                                  ).then_inc(head_done, 1)

            dve.wait_ge(yrs_done, 1)
            for k in range(8):
                dve.scalar_tensor_tensor(t.y[:, k], t.y[:, k], vcol("ssd_norm_g_2", k), t.nt[:, 2 + k // 4], ALU.mult, ALU.mult
                                         ).then_inc(yn_ready, 1)
            dve.drain()
            for k in range(16):
                dve.wait_ge(yhi_done, k + 1)
                dve.tensor_tensor(t.y2lo[:, k], t.y[:, k], t.y2hi[:, k].bitcast(F32), ALU.subtract).then_inc(y2_ready, 1)
            dve.wait_ge(x_back, 16)
            with dve.Fori(0, OUT2_SLOTS // 2) as i:
                for h in range(2):
                    s, m = S_OUT + 2 * i + h, 2 * i + h
                    lo(1 - h, s + 1)
                    dve.wait_ge(slot_done, s + RING + 1)
                    xm = t.x[:, ds(m, 1)].rearrange("p a n -> p (a n)")
                    dve.scalar_tensor_tensor(xm, gemm[:, 2 * h], t.modT[:, ds(20 * KD + m, 1)], xm, ALU.mult, ALU.add
                                             ).then_inc(slot_evicted, 1)
            norm(9, t.x, N, vcol("norm2_g_2", 0, KD), t.modT[:, 22 * KD:23 * KD],
                 lambda k: t.modT[:, 21 * KD + k:21 * KD + k + 1], m=8)
            for half in range(2):
                s0 = S_MLP + 16 * half
                with dve.Fori(0, 4) as i:
                    for h in range(2):
                        s, n = s0 + 2 * i + h, 8 * half + 2 * i + h
                        lo(1 - h, s + 1)
                        dve.drain()
                        dve.wait_ge(rl_done, n + 1)
                        dve.tensor_tensor(t.h2[:], t.rl[:], t.rl[:], ALU.mult).then_inc(h2_ready, 1)
                        dve.sem_inc(slot_evicted, 1)
                        dve.wait_ge(h2hi_done, n + 1)
                        two = ds(4 * i + 2 * h, 2)
                        dve.tensor_tensor(t.hlo[:, two], t.h2[:], t.hhi[:, two].bitcast(F32), ALU.subtract).then_inc(h2_done, 1)
                for m in range(8):
                    s = s0 + 8 + m
                    if not (half and m == 7):
                        lo((m + 1) % 2, s + 1)
                    dve.wait_ge(slot_done, s + RING + 1)
                    dve.scalar_tensor_tensor(t.x[:, m], gemm[:, 2 * (m % 2)], t.modT[:, 23 * KD + m:23 * KD + m + 1], t.x[:, m],
                                             ALU.mult, ALU.add).then_inc(slot_evicted, 1)
            plain(10, "final_g_2", out_ready)

        @block.tensor
        def _(pe):
            pe.wait_ge(init_landed, 16 * INIT)
            pe.drain().then_inc(slot_done, RING)
            pe.drain().then_inc(mod_done, RING)

            def mm3(out, wh, wl, xh, xl, start, stop):
                pe.matmul(out, wh, xh, start=start, stop=False)
                pe.matmul(out, wh, xl, start=False, stop=False)
                return pe.matmul(out, wl, xh, start=False, stop=stop)

            def tile(h, j):
                return t.whi[:, h, P * j:P * j + P], t.wlo[:, h, P * j:P * j + P]

            def enter(s):
                pe.wait_ge(split_done, s + RING + 1)
                pe.wait_ge(slot_evicted, s + 1)

            def mod(c, b):
                pe.wait_ge(ada_acc, c + 1)
                for j in range(2):
                    ins = pe.matmul(pmod[:, ds(2 * c + j, 1)], t.acc[:, b, P * j:P * j + P], t.ones[:, 0:1],
                                    start=True, stop=True)
                ins.then_inc(mod_done, 1)

            def norm(n, tokens):
                for k in range(KD):
                    pe.wait_ge(sq_done, n * KD + k + 1)
                    ins = pe.matmul(misc[:, 0, 0:tokens], t.ones[:], t.sq[:, k, 0:tokens], start=k == 0, stop=k == KD - 1)
                ins.then_inc(ss_done, 1)

            def early_sum(n, k, b, start=False, stop=False):
                pe.wait_ge(sq_done, n * KD + k + 1)
                ins = pe.matmul(misc[:, 0], t.ones[:], t.esq[:, b], start=start, stop=stop)
                if stop:
                    ins.then_inc(ss_done, 1)

            def two_tiles(h, xn):
                for j in range(2):
                    for k in range(KD):
                        if j == 0 and xn is not None:
                            pe.wait_ge(xn_ready, xn + k + 1)
                        ins = mm3(gemm[:, 2 * h + j], *tile(h, KD * j + k), t.xhi[:, k], t.xlo[:, k], k == 0, k == KD - 1)
                ins.then_inc(slot_done, 1)

            def ffn(n, nxt, s0, chunk0, f0, early):
                if early:
                    early_sum(n, KD - 1, KD - 1, stop=True)
                else:
                    norm(n, N)
                with pe.Fori(0, GU_SLOTS // 2) as i:
                    for h in range(2):
                        s = s0 + 2 * i + h
                        enter(s)
                        two_tiles(h, n * KD if h == 0 else None)
                        mod(chunk0 + 2 * i + h, h)

                def down(i, first):
                    for u in range(4):
                        enter(s0 + GU_SLOTS + 4 * i + u)
                        part = u % 2
                        if u == 0:
                            pe.wait_ge(h_ready, (f0 + 1) * GU_SLOTS)
                        for kk in range(HALF):
                            k = part * HALF + kk
                            ins = mm3(gemm[:, u - part], *tile(part, kk), t.hhi[:, k], t.hlo[:, k],
                                      k == 0, k == KF - 1)
                        ins.then_inc(slot_done, 1)
                        if first and u < 2:
                            mod(chunk0 + GU_SLOTS + u, u)
                        if u == 2 or (u == 0 and not first):
                            early_sum(nxt, 2 * i - 1 + u // 2, 1 - u // 2, start=first)

                down(0, True)
                with pe.Fori(1, KD // 2) as i:
                    down(i, False)

            for k in range(KD - 1):
                early_sum(0, k, k, start=k == 0)
            pe.wait_ge(cs_ready, 1)
            for c in range(FIRST_CHUNKS):
                if c % 4 == 0:
                    pe.wait_ge(first_landed[c // 4], 16)
                for j in range(2):
                    for k in range(KD):
                        ins = pe.matmul(pmod[:, 2 * c + j:2 * c + j + 1], t.first[:, c, k, P * j:P * j + P],
                                        t.cs[:, c // 4, k:k + 1], start=k == 0, stop=k == KD - 1)
            ins.then_inc(mod_done, FIRST_CHUNKS)
            pe.drain().then_inc(ada_acc, FIRST_CHUNKS)

            with pe.Fori(0, L) as l:
                s0 = l * LAYER_SLOTS
                chunk0 = FIRST_CHUNKS + 2 * CHUNKS_PER_FFN * l
                ffn(NORMS * l, NORMS * l + 1, s0, chunk0, 2 * l, True)
                s1 = s0 + FFN_SLOTS
                n = NORMS * l + 1
                early_sum(n, KD - 1, KD - 1, stop=True)
                for j in range(IN_SLOTS):
                    enter(s1 + j)
                    two_tiles(j % 2, n * KD if j == 0 else None)
                enter(s1 + IN_SLOTS)
                pe.wait_ge(pool_in, l + 1)
                for g in range(4):
                    out = gemm[:, 2 + g] if g < 2 else misc[:, g - 1]
                    ins = mm3(out, *tile(1, g), t.dif[:, g], t.difl[:, g], True, True)
                ins.then_inc(slot_done, 1)
                pe.wait_ge(c_in, l + 1)
                pe.matmul(misc[:, 0], t.rot[:], t.zin[:, 5], start=True, stop=True).then_inc(rotk_done, 1)
                pe.wait_ge(v_taken, l * (HEADS + 1) + 1)
                pe.wait_ge(slot_evicted, s1 + IN_SLOTS + RING + 1)
                pe.wait_ge(csq_done, l + 1)
                for k in range(5):
                    ins = pe.matmul(misc[:, 0 if k < 3 else 1], t.ones[:], t.msq[:, k], start=k in (0, 3), stop=k in (2, 4))
                ins.then_inc(css_done, 1)
                s2 = s1 + IN_SLOTS + POOL_SLOTS
                with pe.Fori(0, HEADS // 2) as i:
                    for h in range(2):
                        s, hd = s2 + 2 * i + h, l * HEADS + 2 * i + h
                        enter(s)
                        if h == 0:
                            pe.wait_ge(c_ready, l + 1)
                        for k in range(KQ):
                            mm3(gemm[:, 2 * h], *tile(h, k), t.chi[:, k], t.clo[:, k], k == 0, k == KQ - 1)
                        for k in range(KQ):
                            mm3(gemm[:, 2 * h + 1], *tile(h, KQ + k), t.chi[:, k], t.clo[:, k], k == 0, k == KQ - 1)
                        for k in range(KKV):
                            mm3(misc[:, 0], *tile(h, 2 * KQ + k), t.chi[:, KQ + k], t.clo[:, KQ + k], k == 0, k == KKV - 1)
                        for b in range(4):
                            for k in range(KKV):
                                wh, wl = tile(h, 2 * KQ + KKV + k)
                                xh, xl = (v[:, KQ + k, P * b:P * b + P] for v in (t.chi, t.clo))
                                out = misc[:, 1, P * b:P * b + P]
                                pe.matmul(out, xh, wh, start=k == 0, stop=False)
                                pe.matmul(out, xh, wl, start=False, stop=False)
                                ins = pe.matmul(out, xl, wh, start=False, stop=k == KKV - 1)
                        ins.then_inc(slot_done, 1)
                        pe.wait_ge(qr_taken, hd + 1)
                        pe.matmul(misc[:, 2], t.rot[:], t.qr[:], start=True, stop=True).then_inc(rotq_done, 1)
                        pe.wait_ge(kv_taken, hd + 1)
                        pe.wait_ge(qr_ready, hd + 1)

                        def scores(q):
                            if q >= 2:
                                pe.wait_ge(max_ready, hd * 4 + q - 1)
                            bank, keys, cols = misc[:, 2 * (q % 2)], P * (q + 1), slice(P * q, P * q + P)
                            pe.matmul(bank[:, 0:keys], t.qn[:, cols], t.kn[:, 0:keys], start=True, stop=False)
                            pe.matmul(bank[:, 0:keys], t.qr[0:ROPE, cols], t.krr[0:ROPE, 0:keys], start=False,
                                      stop=True).then_inc(sc_done, 1)

                        scores(0)
                        for q in range(4):
                            if q < 3:
                                scores(q + 1)
                            u = hd * 4 + q
                            pe.wait_ge(p_ready, u + 1)
                            if q:
                                pe.wait_ge(pT_taken, u)
                            for b in range(q + 1):
                                ins = pe.transpose(gemm[:, 2 * h, P * b:P * b + P], t.pr[:, q % 2, P * b:P * b + P], t.ident[:])
                            ins.then_inc(pT_done, 1)
                            pe.wait_ge(pT_taken, u + 1)
                            for b in range(q + 1):
                                ins = pe.matmul(gemm[:, 2 * h + 1, P * q:P * q + P], t.vt[:, b], t.pT[:, b],
                                                start=b == 0, stop=b == q)
                        ins.then_inc(o_done, 1)
                s3 = s2 + HEADS
                with pe.Fori(0, OUT_SLOTS // 2) as i:
                    for h in range(2):
                        s = s3 + 2 * i + h
                        enter(s)
                        if h == 0:
                            pe.wait_ge(slot_evicted, s3 + RING)
                        for j in range(2):
                            for k in range(KD):
                                ins = mm3(gemm[:, 2 * h + j], *tile(h, KD * j + k), t.yhi[:, k], t.ylo[:, k],
                                          k == 0, k == KD - 1)
                        ins.then_inc(slot_done, 1)
                ffn(NORMS * l + 2, NORMS * l + 3, s3 + OUT_SLOTS, chunk0 + CHUNKS_PER_FFN, 2 * l + 1, False)

            early_sum(6, KD - 1, KD - 1, stop=True)
            norm(7, N)
            norm(8, CT)

            def lat_ctx(h, s, ctx_tiles, tiles=2, first=False):
                pe.wait_ge(split_done, s + RING + 1)
                pe.wait_ge(slot_evicted, s + RING)
                if first:
                    pe.wait_ge(xn_ready, 8 * KD)
                for j in range(tiles):
                    for k in range(KD):
                        ins = mm3(gemm[:, j], *tile(h, KD * j + k), t.xhi[:, k], t.xlo[:, k], k == 0, k == KD - 1)
                    if j in ctx_tiles:
                        for k in range(KD):
                            ins = mm3(gemm[:, 2, CT * j:CT * j + CT], *tile(h, KD * j + k), t.c2hi[:, k], t.c2lo[:, k],
                                      k == 0, k == KD - 1)
                ins.then_inc(slot_done, 1)

            def quarter(h, s, n):
                if n == 0:
                    pe.wait_ge(split_done, s + RING + 1)
                    pe.wait_ge(slot_evicted, s + RING)
                for k in (2 * n, 2 * n + 1):
                    for j in range(2):
                        mm3(gemm[:, j], *tile(h, KD * j + k), t.xhi[:, k], t.xlo[:, k], k == 0, k == KD - 1)
                    ins = mm3(gemm[:, 2, 0:CT], *tile(h, k), t.c2hi[:, k], t.c2lo[:, k], k == 0, k == KD - 1)
                if n == 3:
                    ins.then_inc(slot_done, 1)

            def turn(outs, src, n=P, m=P):
                for c in range(NC_ALL):
                    out = outs[0][:, P * c:P * c + P] if c < 4 else outs[1][:, P * (c - 4):P * (c - 4) + P]
                    ins = pe.transpose(out, src(c), t.ident[:])
                return ins

            def three(out, b, f):
                for c in range(3):
                    l, r = f(3 * b + c)
                    ins = pe.matmul(out[:, P * c:P * c + P], l, r, start=True, stop=True)
                return ins

            def six(outs, f):
                for c in range(NC_ALL):
                    out = outs[0][:, P * c:P * c + P] if c < 4 else outs[1][:, P * (c - 4):P * (c - 4) + P]
                    l, r = f(c)
                    ins = pe.matmul(out, l, r, start=True, stop=True)
                return ins

            lat_ctx(0, SB, (0, 1), first=True)
            lat_ctx(1, SB + 1, (0,), tiles=1)
            pe.wait_ge(act_done, 2)
            turn((work[0], work[1]), lambda c: t.bf[:, P * c:P * c + P])
            for g in range(2):
                G = slice(64 * g, 64 * g + 64)
                for c in range(NC_LAT):
                    q = slice(P * c, P * c + P)
                    ins = pe.matmul(work[2 + g][:, q], t.bf[G, q], t.cf[G, q], start=True, stop=True)
            ins.then_inc(bc_done, 1)
            pe.wait_ge(bc_taken, 1)
            pe.wait_ge(f_ready, 1)
            for c in range(NC_ALL):
                q = slice(P * c, P * c + P)
                pe.transpose(work[c // 3][:, 96 * (c % 3):96 * (c % 3) + 96], t.f1[0:96, q], t.ident[0:96, 0:96])
                ins = pe.transpose(work[2][:, 64 * c:64 * c + 64], t.f2[0:64, q], t.ident[0:64, 0:64])
            ins.then_inc(ft_done, 1)
            pe.wait_ge(tm_ready, 1)
            for d in range(2):
                pe.matmul(work[0][:, 96 * d:96 * d + 96].rearrange("p (c h) -> p c h", c=NC_ALL), t.tri[:, d],
                          t.tm2[:, :, 16 * d:16 * d + 16], start=True, stop=True)
            pe.matmul(work[0][:, 192:384].rearrange("p (c h) -> p c h", c=NC_ALL), t.ones[:], t.tm2[:, :, 0:32],
                      start=True, stop=True)
            for d in range(2):
                pe.matmul(work[1][:, 48 * d:48 * d + 48].rearrange("p (c h) -> p c h", c=NC_ALL), t.tri[:, 2 + d],
                          t.tm2[:, :, 32 + 8 * d:40 + 8 * d], start=True, stop=True)
            for n in range(3):
                ins = pe.matmul(work[1][:, 96 + 96 * n:192 + 96 * n].rearrange("p (c h) -> p c h", c=NC_ALL), t.tri[:, 4 + n],
                                t.tm2[:, :, 32:48], start=True, stop=True)
            ins.then_inc(cum_done, 1)
            pe.wait_ge(cum_taken, 1)
            for d in range(2):
                if d:
                    pe.wait_ge(hm_taken, 1)
                for c in range(NC_ALL):
                    q = slice(P * c, P * c + P)
                    if c < NC_LAT:
                        pe.matmul(work[0][0:16, q], t.tm2[:, c, 16 * d:16 * d + 16], t.tri[:, d], start=True, stop=True)
                    out = work[1][0:8, q] if c < 4 else work[2][0:8, P * (c - 4):P * (c - 4) + P]
                    ins = pe.matmul(out, t.tm2[:, c, 32 + 8 * d:40 + 8 * d], t.tri[:, 2 + d], start=True, stop=True)
                ins.then_inc(hm_done, 1)

            lat_ctx(0, SB + 2, (0,))
            with pe.Fori(0, PAIRS // 2) as i:
                for g in range(2):
                    u, k = 2 * i + g, 4 * g + i
                    s = SB + 2 + u
                    G = slice(64 * g, 64 * g + 64)
                    pe.wait_ge(hm_taken, 2)
                    pe.wait_ge(act_done, 3 + u)
                    turn((work[0], work[1]), lambda c: t.xa[:, P * c:P * c + P]).then_inc(xt_done, 1)
                    pe.wait_ge(wx_ready, u + 1)
                    for d in range(2):
                        if d:
                            pe.wait_ge(hp_ready, 2 * u + 1)
                        for c in ORDER[d][0:5]:
                            out = work[0][G, P * c:P * c + P] if c < 4 else work[1][G, P * (c - 4):P * (c - 4) + P]
                            ins = pe.matmul(out, t.btm[:, c, G], t.wx[:, d, c], start=True, stop=True)
                        ins.then_inc(st_done, 1)
                    pe.wait_ge(sel_ready, 2 * u + 2)
                    pe.wait_ge(pair_done, u + 1)

                    def row(r):
                        pe.matmul(work[2 + r % 2], t.sel[:, r // 2], t.ahm[:, r % 2], start=True, stop=True).then_inc(row_done, 1)

                    row(0)
                    for r in range(4):
                        e, d = r // 2, r % 2
                        v = 4 * u + r
                        if r < 3:
                            row(r + 1)
                        quarter(1 - g, s + 1, r)
                        pe.wait_ge(es_ready, v + 1)
                        if r == 0:
                            pe.wait_ge(xdt_ready, u + 1)
                            pe.wait_ge(hp_ready, 2 * u + 2)
                        E = slice(64 * e, 64 * e + 64)
                        for c in range(NC_LAT):
                            q = slice(P * c, P * c + P)
                            pe.matmul(work[4][E, q], t.xdt[:, d, c, E], t.es[:, q], start=(d == 0 and c == 0), stop=False,
                                      skip_group_check=True)
                            ins = pe.matmul(work[4][E, q], t.hp[G, d, ORDER[d].index(c) - 1, E], t.cpr[G, q],
                                            start=False, stop=True, skip_group_check=True)
                        ins.then_inc(yc_done, 1)

            def gdn_head(hd, last):
                s = SB + 2 + PAIRS + 2 * hd
                lat_ctx(1, s + 1, (0,))
                pe.wait_ge(pair_done, PAIRS + 1)
                pe.wait_ge(g_sq, hd + 1)
                pe.matmul(work[0], t.ones[:], t.gsq[:, 0, 0:N], start=True, stop=True)
                pe.matmul(work[1], t.ones[:], t.gsq[:, 1, 0:N], start=True, stop=True)
                pe.matmul(work[2][:, 0:CT], t.ones[:], t.gsq[:, 1, N:N + CT], start=True, stop=True).then_inc(g_ss, 1)
                pe.wait_ge(g_rs, hd + 1)
                turn((work[2], work[3]), lambda c: t.gv[:, P * c:P * c + P]).then_inc(g_vt, 1)
                pe.wait_ge(g_hat, hd + 1)
                turn((work[0], work[1]), lambda c: t.gk[:, P * c:P * c + P]).then_inc(g_kt, 1)
                pe.wait_ge(g_vtm, hd + 1)
                six((work[2], work[3]), lambda c: (t.gk[:, P * c:P * c + P],) * 2)
                for c in range(NC_LAT):
                    q = slice(P * c, P * c + P)
                    ins = pe.matmul(work[4][:, q], t.gk[:, q], t.gq[:, q], start=True, stop=True)
                ins.then_inc(g_kk, 1)
                pe.wait_ge(g_ktm, hd + 1)
                for d in range(2):
                    v = 2 * hd + d
                    pe.wait_ge(g_sel, v + 1)
                    if d:
                        pe.wait_ge(g_u, v)
                    pe.matmul(work[0], t.sel8[:], t.ghm[:, d, 0:N], start=True, stop=True)
                    pe.matmul(work[1][:, 0:CT], t.sel8[:], t.ghm[:, d, N:N + CT], start=True, stop=True).then_inc(g_row, 1)
                    if d == 0 and not last:
                        quarter(0, s + 2, 0)
                        quarter(0, s + 2, 1)
                    if d == 1 and not last:
                        quarter(0, s + 2, 2)
                        quarter(0, s + 2, 3)
                    pe.wait_ge(g_A, v + 1)
                    for b in range(2):
                        for c in range(3):
                            ins = pe.transpose(work[b][:, P * c:P * c + P], t.A[:, 3 * b + c], t.ident[:])
                    ins.then_inc(g_At, 1)
                    for n in range(NLV):
                        q = 2 * (v * NLV + n)
                        for b in range(2):
                            pe.wait_ge(g_X, 2 * v * (NLV + 1) + 2 * n + b + 1)
                            three(work[b], b, lambda c: (t.A[:, c], t.X[:, c])).then_inc(g_e, 1)
                        for b in range(2):
                            pe.wait_ge(g_es, q + b + 1)
                            if n < NLV - 1:
                                three(work[2 + b], b, lambda c: (t.Xt[:, c], t.E[:, c]))
                            three(work[b], b, lambda c: (t.E[:, c], t.Xt[:, c])).then_inc(g_xe, 1)
                    pe.wait_ge(g_X, 2 * (v + 1) * (NLV + 1))
                    pe.wait_ge(g_ke, v + 1)
                    for b in range(2):
                        three(work[b], b, lambda c: (t.Xt[:, c], t.vtm[:, c]))
                        ins = three(work[2 + b], b, lambda c: (t.dec[:, c], t.Xt[:, c]))
                    ins.then_inc(g_uw, 1)
                pe.wait_ge(g_u, 2 * hd + 2)
                pe.wait_ge(g_w, 2 * hd + 2)
                for n in range(NST):
                    if n:
                        for d in range(2):
                            c, b = STEPS[d][n]
                            H = slice(Q64 * b, Q64 * b + Q64)
                            pe.wait_ge(g_S, 2 * (NST - 1) * hd + 2 * (n - 1) + d + 1)
                            pe.matmul(work[d][H, 0:P], (t.w0, t.X)[d][:, c, H], t.S[:, d, 1 - n % 2], start=True,
                                      stop=True).then_inc(g_p, 1)
                    for d in range(2):
                        c, b = STEPS[d][n]
                        H = slice(Q64 * b, Q64 * b + Q64)
                        q = slice(P * c + Q64 * b, P * c + Q64 * b + Q64)
                        if c < NC_LAT:
                            pe.matmul(work[4][:, q], t.S[:, d, 1 - n % 2], (t.qdec, t.gq)[d][:, q],
                                      start=(d == 0 and n == 4), stop=False, skip_group_check=True)
                        pe.wait_ge(g_vn, 2 * NST * hd + 2 * n + d + 1)
                        if n < NST - 1:
                            pe.matmul(work[2 + d][:, 0:P], (t.kdec, t.kk)[d][H, c], t.vn[H, d], start=True,
                                      stop=True).then_inc(g_sd, 1)
                        if c < NC_LAT:
                            ins = pe.matmul(work[4][:, q], t.vn[:, d], (t.qkd, t.qk)[d][:, c, H], start=False, stop=True,
                                            skip_group_check=True)
                ins.then_inc(g_o, 1)
                pe.wait_ge(g_osq, hd + 1)
                pe.matmul(work[0], t.ones[:], t.E[:, 0:4].rearrange("p c n -> p (c n)"), start=True, stop=True).then_inc(g_oss, 1)

            with pe.Fori(0, GDN_H - 1) as hd:
                gdn_head(hd, False)
            gdn_head(GDN_H - 1, True)

            for g in range(2):
                for k in range(4):
                    pe.wait_ge(ysq_done, 4 * g + k + 1)
                    ins = pe.matmul(work[g], t.ones[:], t.sq[:, 4 * g + k], start=k == 0, stop=k == 3)
            ins.then_inc(yss_done, 1)
            with pe.Fori(0, OUT2_SLOTS // 2) as i:
                for h in range(2):
                    enter(S_OUT + 2 * i + h)
                    for k in range(16):
                        if h == 0:
                            pe.wait_ge(y2_ready, k + 1)
                        ins = mm3(gemm[:, 2 * h], *tile(h, k), t.y2hi[:, k], t.y2lo[:, k], k == 0, k == 15)
                    ins.then_inc(slot_done, 1)
            norm(9, N)
            for half in range(2):
                s0 = S_MLP + 16 * half
                with pe.Fori(0, 4) as i:
                    for h in range(2):
                        enter(s0 + 2 * i + h)
                        two_tiles(h, 8 * KD if h == 0 else None)
                with pe.Fori(0, 4) as i:
                    for h in range(2):
                        enter(s0 + 8 + 2 * i + h)
                        if h == 0:
                            pe.wait_ge(h2_done, 8 * (half + 1))
                        for k in range(16):
                            ins = mm3(gemm[:, 2 * h], *tile(h, k), t.hhi[:, k], t.hlo[:, k], k == 0, k == 15)
                        ins.then_inc(slot_done, 1)
            norm(10, N)


def tiles_of(w, k, m):
    l = w.shape[0]
    return w.reshape(l, k, P, m, P).transpose(0, 3, 2, 1, 4)


def lay(inputs):
    f = {}
    I = {k: np.asarray(v) for k, v in inputs.items()}
    fm = lambda v: np.ascontiguousarray(v.T.reshape(KD, P, -1).transpose(1, 0, 2))
    f["x"] = fm(I["x"][0])
    col = lambda v: v.reshape(-1, P).T
    f["c"] = np.ascontiguousarray(np.stack([col(I["c"][0]), col(I["c_2"][0]), col(I["c_ctx_2"])], 1))
    for j in (1, 2):
        g, u = (tiles_of(I[f"ffn{j}_w_{n}"], KD, KF) for n in ("gate", "up"))
        f[f"gu{j}"] = np.stack([g, u], 3).reshape(L * KF, P, 16 * P)
        dn = tiles_of(I[f"ffn{j}_w_down"], KF, KD).reshape(L, KD, P, 2, HALF * P).transpose(0, 1, 3, 2, 4)
        f[f"down{j}"] = np.ascontiguousarray(dn.reshape(L * DOWN_SLOTS, P, HALF * P))
    w = np.concatenate([I["w_in"], I["w_in"][:, :, -ROPE:]], 2)
    w = tiles_of(w, KD, 10).reshape(L, 5, 2, P, KD * P).transpose(0, 1, 3, 2, 4)
    f["w_in"] = np.ascontiguousarray(w.reshape(L * IN_SLOTS, P, 16 * P))
    f["pool_w"] = np.ascontiguousarray(I["pool_w"].transpose(0, 2, 1, 3).reshape(L, P, 4 * P))
    q = I["w_q_b"].reshape(L, KQ, P, HEADS, NOPE + ROPE).transpose(0, 3, 2, 1, 4)
    kv = I["w_kv_b"].reshape(L, KKV, P, HEADS, NOPE + DV).transpose(0, 3, 2, 1, 4)
    parts = [q[..., :NOPE], np.concatenate([q[..., NOPE:], q[..., NOPE:]], -1), kv[..., :NOPE], kv[..., NOPE:]]
    f["head_w"] = np.concatenate([p.reshape(L * HEADS, P, -1) for p in parts], 2)
    w = tiles_of(I["w_out"], KD, KD).reshape(L, OUT_SLOTS, 2, P, KD * P).transpose(0, 1, 3, 2, 4)
    f["w_out"] = np.ascontiguousarray(w.reshape(L * OUT_SLOTS, P, 16 * P))
    ada = [I["ada_w"][0], I["ada_w"][1], I["w_mod_2"][0], I["w_mod_2"][0][:, :2 * D], I["w_mod_2"][0][:, D:2 * D]]
    ada = np.concatenate(ada, 1).reshape(KD, P, N_CHUNKS, 256).transpose(2, 1, 0, 3)
    f["ada"] = np.ascontiguousarray(ada.reshape(N_CHUNKS, P, KD * 256))
    b2 = I["b_mod_2"][0]
    b = np.concatenate([I["ada_b"][0], I["ada_b"][1], b2, b2[:2 * D], b2[D:2 * D]])
    f["ada_b"] = np.ascontiguousarray(col(b))
    I["ssd_D_2"] = np.repeat(I["ssd_D_2"][0], SSD_P)
    for n in ("ssd", "gdn"):
        v = I[f"{n}_conv_w_2"][0]
        I[f"{n}_conv_w_2"] = v.reshape(CW, -1, P).transpose(1, 0, 2)
    pad = np.zeros(P - 48, np.float32)
    I["dt_bias_2"] = np.concatenate([I["ssd_dt_bias_2"].reshape(-1), I["gdn_dt_bias_2"].reshape(-1), pad])
    I["A_log_2"] = np.concatenate([I["ssd_A_log_2"].reshape(-1), I["gdn_A_log_2"].reshape(-1), pad])
    f["vec"] = np.ascontiguousarray(np.concatenate([col(I[n].reshape(-1)) for n in VEC], 1))
    f["ctx"] = np.ascontiguousarray(I["ctx_2"][0].T.reshape(KD, P, CT).transpose(1, 0, 2))
    w = I["w_in_2"][0]
    z, xs, bb, cc, dt, qkv, gate, ga, gb = np.split(w, np.cumsum([1024, 1024, 128, 128, 32, 3072, 1024, 16]), 1)
    zero = lambda n: np.zeros((D, n), np.float32)
    cols = [bb, cc, dt, ga, zero(16), gb, zero(48), zero(P)]
    of = lambda v, k: v[:, P * k:P * k + P]
    for i in range(4):
        for g in range(2):
            cols += [of(xs, 4 * g + i), of(z, 4 * g + i)]
    for h in range(GDN_H):
        cols += [of(qkv, 8 + h), of(qkv, h), of(qkv, 16 + h), of(gate, h)]
    w = tiles_of(np.concatenate(cols, 1)[None], KD, 2 * IN2_SLOTS)[0]
    pairs = lambda w: np.ascontiguousarray(w.reshape(-1, 2, P, KD * P).transpose(0, 2, 1, 3).reshape(-1, P, 16 * P))
    f["w_in2"] = pairs(w)
    f["w_out2"] = np.ascontiguousarray(tiles_of(I["w_out_2"], 16, KD)[0].reshape(KD, P, 16 * P))
    f["up2"] = pairs(tiles_of(I["w_mlp1_2"], KD, 32)[0])
    w = tiles_of(I["w_mlp2_2"].reshape(2, F2 // 2, D), 16, KD)
    f["down2b"] = np.ascontiguousarray(w.reshape(16, P, 16 * P))
    f["pos"] = I["positions"][0]
    f["ident"] = np.eye(P, dtype=np.float32)
    f["ones"] = np.ones((P, P), np.float32)
    r = np.zeros((P, P), np.float32)
    for o in (0, ROPE):
        for i in range(ROPE // 2):
            r[o + ROPE // 2 + i, o + i] = -1
            r[o + i, o + ROPE // 2 + i] = 1
    f["rot"] = r
    i = np.arange(P)
    f["dmask"] = np.where(i[:, None] >= i[None, :], 0, NEG).astype(np.float32)
    inv = (1.0 / (np.float32(THETA) ** (np.arange(0, ROPE, 2, dtype=np.float32) / np.float32(ROPE)))).astype(np.float32)
    f["freq"] = np.tile(inv, 4)[:, None].copy()
    n = np.arange(PAD)
    f["pfac"] = np.ascontiguousarray(np.broadcast_to(
        np.stack([w / np.minimum(n + 1, w) for w in POOL_WINDOWS]).astype(np.float32), (P, 4, PAD)))
    j = np.arange(P)[:, None]
    i = np.arange(P)[None, :]
    same = j // Q64 == i // Q64
    tri = [j <= i, j >= i, same & (j <= i), same & (j >= i), same, (j < Q64) & (i >= 0), (j >= Q64) & (i >= 0)]
    stack = lambda v: np.ascontiguousarray(np.stack(v, 1).astype(np.float32))
    f["tri"] = stack(tri)
    f["neg"] = stack([np.where(v, 0, NEG) for v in tri[:4]])
    later = [(j // (2 * b) == i // (2 * b)) & (j // b % 2 == 1) & (i // b % 2 == 0) for b in LEVELS]
    f["lev"] = stack(later + [v.T for v in later])
    f["eps"] = np.full((P, 1), EPS, np.float32)
    return f


INPUTS = ("x", "c", "gu1", "down1", "gu2", "down2", "w_in", "pool_w", "head_w", "w_out", "ada", "ada_b", "vec", "pos",
          "ctx", "w_in2", "w_out2", "up2", "down2b", "ident", "ones", "rot", "dmask", "freq", "pfac", "tri", "neg", "lev",
          "eps")


def kernel(**inputs):
    import concourse.bacc as bacc
    from concourse.bass_utils import run_bass_kernel_spmd

    f = lay(inputs)
    nc = bacc.Bacc("TRN2", target_bir_lowering=False, num_devices=1)
    a = Names()
    arrays = {f"in_{name}": np.ascontiguousarray(f[name]) for name in INPUTS}
    (a.x, a.c, a.gu1, a.down1, a.gu2, a.down2, a.w_in, a.pool_w, a.head_w, a.w_out, a.ada, a.ada_b, a.vec, a.pos,
     a.ctx, a.w_in2, a.w_out2, a.up2, a.down2b, a.ident, a.ones, a.rot, a.dmask, a.freq, a.pfac, a.tri, a.neg, a.lev,
     a.eps) = (nc.dram_tensor(n, v.shape, mybir.dt.from_np(v.dtype), kind="ExternalInput").ap() for n, v in arrays.items())
    a.out = nc.dram_tensor("out_x", (P, KD, N), F32, kind="ExternalOutput").ap()
    build(nc, a)
    out = run_bass_kernel_spmd(nc, [arrays], core_ids=[0]).results[0]["out_x"]
    return np.ascontiguousarray(out.transpose(1, 0, 2).reshape(D, N).T)[None]
```
